# Optimizing a Trainium2 kernel written in Bass

```python
import math
import jax, jax.numpy as jnp
from jax import lax
import numpy as np

D_MODEL = 1024
BATCH = 1
SEQ = 512
DEPTH = 2

N_MEM = 256
N_HEADS = 4
HEAD_DIM = 64
BRANCH_W = N_HEADS * HEAD_DIM
N_BRANCH = 5
ROPE_THETA = 500000.0
ROT_64 = 16
ROT_32 = 8
Q_BLOCK = 128
IDX_HEADS = 8
IDX_DIM = 32
TOPK_MAX = 256
MOBA_BLOCK = 256
MOBA_TOPK = 3
MOBA_Q_CHUNK = 64
DIFF_DIM = 32
Q_LORA = 256
KV_LORA = 128
MLA_NOPE = 64
MLA_ROPE = 32
MLA_V = 64
DN_ALPHA = (2 * DEPTH) ** 0.25
DN_BETA = (8 * DEPTH) ** -0.25
LN_EPS = 1e-5
RMS_EPS = 1e-6

IN_LAYOUT = (
    ("a_q", BRANCH_W), ("a_k", BRANCH_W), ("a_v", BRANCH_W),
    ("i_q", IDX_HEADS * IDX_DIM), ("i_k", IDX_DIM), ("i_w", IDX_HEADS),
    ("b_q", BRANCH_W), ("b_k", BRANCH_W), ("b_v", BRANCH_W),
    ("c_q", BRANCH_W), ("c_k", BRANCH_W), ("c_v", BRANCH_W),
    ("d_cq", Q_LORA), ("d_ckv", KV_LORA), ("d_kr", MLA_ROPE),
    ("e_q", BRANCH_W),
    ("z", N_BRANCH * BRANCH_W),
    ("g", N_BRANCH * D_MODEL),
)
IN_WIDTH = sum(s for _, s in IN_LAYOUT)

kernel_name = "hybrid_gated_dsa_moba_diff_mla_mem_deepnorm"

def split_projection(h):
    sizes = [s for _, s in IN_LAYOUT]
    offsets = [int(o) for o in np.cumsum(sizes)[:-1]]
    parts = jnp.split(h, offsets, axis=-1)
    return {name: p for (name, _), p in zip(IN_LAYOUT, parts)}

def layer_norm(x, g, b):
    xf = x.astype(jnp.float32)
    mu = jnp.mean(xf, -1, keepdims=True)
    var = jnp.mean(jnp.square(xf - mu), -1, keepdims=True)
    return ((xf - mu) * lax.rsqrt(var + LN_EPS) * g + b).astype(x.dtype)

def rms_norm(x, g):
    xf = x.astype(jnp.float32)
    return (xf * lax.rsqrt(jnp.mean(jnp.square(xf), -1, keepdims=True) + RMS_EPS) * g).astype(x.dtype)

def rope_tables(seq, rot_dim):
    pos = jnp.arange(seq, dtype=jnp.float32)
    inv = ROPE_THETA ** (-jnp.arange(0, rot_dim, 2, dtype=jnp.float32) / rot_dim)
    ang = pos[:, None] * inv[None, :]
    return jnp.cos(ang), jnp.sin(ang)

def apply_rope(x, cos, sin):
    half = x.shape[-1] // 2
    x1, x2 = x[..., :half], x[..., half:]
    c = cos[None, :, None, :].astype(x.dtype)
    s = sin[None, :, None, :].astype(x.dtype)
    return jnp.concatenate([x1 * c - x2 * s, x2 * c + x1 * s], -1)

def partial_rope(x, cos, sin):
    r = 2 * cos.shape[-1]
    return jnp.concatenate([apply_rope(x[..., :r], cos, sin), x[..., r:]], -1)

def to_blocks(x, blk):
    b, t = x.shape[:2]
    return jnp.moveaxis(x.reshape((b, t // blk, blk) + x.shape[2:]), 1, 0)

def from_blocks(y):
    y = jnp.moveaxis(y, 0, 1)
    return y.reshape((y.shape[0], -1) + y.shape[3:])

def sweep(fn, qs, blk):
    t = qs[0].shape[1]
    starts = jnp.arange(t // blk, dtype=jnp.int32) * blk
    out = lax.map(lambda a: fn(a[0], *a[1:]), (starts,) + tuple(to_blocks(q, blk) for q in qs))
    return from_blocks(out)

def dsa_attention(q, k, v, qi, ki, wi):
    b, t = q.shape[:2]
    topk = min(TOPK_MAX, t // 4)
    kpos = jnp.arange(t)
    bidx = jnp.arange(b)[:, None, None]
    scale = HEAD_DIM ** -0.5
    idx_scale = (IDX_HEADS * IDX_DIM) ** -0.5

    def block(start, qb, qib, wib):
        qpos = start + jnp.arange(Q_BLOCK)
        causal = kpos[None, :] <= qpos[:, None]
        logits = jnp.einsum('bqhd,bkd->bqhk', qib, ki)
        score = jnp.einsum('bqhk,bqh->bqk', jax.nn.relu(logits), wib).astype(jnp.float32) * idx_scale
        score = jnp.where(causal[None], score, -jnp.inf)
        _, sel = lax.top_k(score, topk)
        valid = sel <= qpos[None, :, None]
        kg = k[bidx, sel]
        vg = v[bidx, sel]
        s = jnp.einsum('bqhd,bqkhd->bqhk', qb, kg).astype(jnp.float32) * scale
        s = jnp.where(valid[:, :, None, :], s, -jnp.inf)
        p = jax.nn.softmax(s, axis=-1).astype(v.dtype)
        return jnp.einsum('bqhk,bqkhd->bqhd', p, vg)

    return sweep(block, (q, qi, wi), Q_BLOCK)

def moba_attention(q, k, v):
    b, t, h, dh = q.shape
    nb = -(-t // MOBA_BLOCK)
    n_sel = min(MOBA_TOPK, nb - 1)
    pad = nb * MOBA_BLOCK - t
    kp = jnp.pad(k, ((0, 0), (0, pad), (0, 0), (0, 0)))
    vp = jnp.pad(v, ((0, 0), (0, pad), (0, 0), (0, 0)))
    kb = kp.reshape(b, nb, MOBA_BLOCK, h, dh)
    vb = vp.reshape(b, nb, MOBA_BLOCK, h, dh)
    kbar = jnp.mean(kb, axis=2)
    kbh = jnp.moveaxis(kb, 3, 1)
    vbh = jnp.moveaxis(vb, 3, 1)
    bidx = jnp.arange(b)[:, None, None, None]
    hidx = jnp.arange(h)[None, None, :, None]
    blk_ids = jnp.arange(nb)
    own_off = jnp.arange(MOBA_BLOCK)
    scale = dh ** -0.5

    def block(start, qb):
        nq = qb.shape[1]
        qpos = start + jnp.arange(nq)
        own = start // MOBA_BLOCK
        k_own = lax.dynamic_slice_in_dim(kp, own * MOBA_BLOCK, MOBA_BLOCK, axis=1)
        v_own = lax.dynamic_slice_in_dim(vp, own * MOBA_BLOCK, MOBA_BLOCK, axis=1)
        own_pos = own * MOBA_BLOCK + own_off
        s_own = jnp.einsum('bqhd,bjhd->bqhj', qb, k_own).astype(jnp.float32) * scale
        s_own = jnp.where((own_pos[None, :] <= qpos[:, None])[None, :, None, :], s_own, -jnp.inf)
        if n_sel == 0:
            p = jax.nn.softmax(s_own, axis=-1).astype(v.dtype)
            return jnp.einsum('bqhj,bjhd->bqhd', p, v_own)
        gate = jnp.einsum('bqhd,bnhd->bqhn', qb, kbar).astype(jnp.float32)
        gate = jnp.where(blk_ids < own, gate, -jnp.inf)
        _, sel = lax.top_k(gate, n_sel)
        sel_valid = sel < own
        kg = kbh[bidx, hidx, sel]
        vg = vbh[bidx, hidx, sel]
        s_sel = jnp.einsum('bqhd,bqhsjd->bqhsj', qb, kg).astype(jnp.float32) * scale
        s_sel = jnp.where(sel_valid[..., None], s_sel, -jnp.inf).reshape(b, nq, h, n_sel * MOBA_BLOCK)
        p = jax.nn.softmax(jnp.concatenate([s_sel, s_own], -1), axis=-1).astype(v.dtype)
        p_sel = p[..., :n_sel * MOBA_BLOCK].reshape(b, nq, h, n_sel, MOBA_BLOCK)
        p_own = p[..., n_sel * MOBA_BLOCK:]
        return (jnp.einsum('bqhsj,bqhsjd->bqhd', p_sel, vg)
                + jnp.einsum('bqhj,bjhd->bqhd', p_own, v_own))

    return sweep(block, (q,), MOBA_Q_CHUNK)

def diff_attention(q, k, v, lam):
    t = q.shape[1]
    kpos = jnp.arange(t)
    scale = DIFF_DIM ** -0.5

    def block(start, qb):
        qpos = start + jnp.arange(Q_BLOCK)
        causal = kpos[None, :] <= qpos[:, None]
        s = jnp.einsum('bqhcd,bkhcd->bhcqk', qb, k).astype(jnp.float32) * scale
        p = jax.nn.softmax(jnp.where(causal, s, -jnp.inf), axis=-1)
        pd = (p[:, :, 0] - lam * p[:, :, 1]).astype(v.dtype)
        return jnp.einsum('bhqk,bkhd->bqhd', pd, v)

    return sweep(block, (q,), Q_BLOCK)

def mla_attention(qn, qr, kn, kr, v):
    t = qn.shape[1]
    kpos = jnp.arange(t)
    scale = (MLA_NOPE + MLA_ROPE) ** -0.5

    def block(start, qnb, qrb):
        qpos = start + jnp.arange(Q_BLOCK)
        causal = kpos[None, :] <= qpos[:, None]
        s = (jnp.einsum('bqhd,bkhd->bhqk', qnb, kn)
             + jnp.einsum('bqhr,bkr->bhqk', qrb, kr)).astype(jnp.float32) * scale
        p = jax.nn.softmax(jnp.where(causal, s, -jnp.inf), axis=-1).astype(v.dtype)
        return jnp.einsum('bhqk,bkhd->bqhd', p, v)

    return sweep(block, (qn, qr), Q_BLOCK)

def memory_attention(q, mk, mv):
    s = jnp.einsum('bthd,bmhd->bhtm', q, mk).astype(jnp.float32) * HEAD_DIM ** -0.5
    p = jax.nn.softmax(s, axis=-1).astype(mv.dtype)
    return jnp.einsum('bhtm,bmhd->bthd', p, mv)

def hybrid_layer(x, mem, rot64, rot32, rot_mla, layer_idx, w_in, mla_q_norm, w_uq, mla_kv_norm,
                 w_ukv, diff_lam, diff_norm, w_mem_kv, w_branch, w_out, ln_g, ln_b):
    b, t, d = x.shape
    pr = split_projection(x @ w_in)

    def heads(a, n, dd):
        return a.reshape(b, t, n, dd)

    aq = partial_rope(heads(pr['a_q'], N_HEADS, HEAD_DIM), *rot64)
    ak = partial_rope(heads(pr['a_k'], N_HEADS, HEAD_DIM), *rot64)
    av = heads(pr['a_v'], N_HEADS, HEAD_DIM)
    iq = partial_rope(heads(pr['i_q'], IDX_HEADS, IDX_DIM), *rot32)
    ik = partial_rope(pr['i_k'][:, :, None, :], *rot32)[:, :, 0]
    o_a = dsa_attention(aq, ak, av, iq, ik, pr['i_w'])

    bq = partial_rope(heads(pr['b_q'], N_HEADS, HEAD_DIM), *rot64)
    bk = partial_rope(heads(pr['b_k'], N_HEADS, HEAD_DIM), *rot64)
    o_b = moba_attention(bq, bk, heads(pr['b_v'], N_HEADS, HEAD_DIM))

    cq = partial_rope(heads(pr['c_q'], 2 * N_HEADS, DIFF_DIM), *rot32).reshape(b, t, N_HEADS, 2, DIFF_DIM)
    ck = partial_rope(heads(pr['c_k'], 2 * N_HEADS, DIFF_DIM), *rot32).reshape(b, t, N_HEADS, 2, DIFF_DIM)
    cv = heads(pr['c_v'], N_HEADS, 2 * DIFF_DIM)
    lam_init = 0.8 - 0.6 * math.exp(-0.3 * layer_idx)
    dl = diff_lam.astype(jnp.float32)
    lam = jnp.exp(jnp.sum(dl[0] * dl[1])) - jnp.exp(jnp.sum(dl[2] * dl[3])) + lam_init
    o_c = rms_norm(diff_attention(cq, ck, cv, lam), diff_norm) * (1.0 - lam_init)

    q_full = (rms_norm(pr['d_cq'], mla_q_norm) @ w_uq).reshape(b, t, N_HEADS, MLA_NOPE + MLA_ROPE)
    qn, qr = q_full[..., :MLA_NOPE], apply_rope(q_full[..., MLA_NOPE:], *rot_mla)
    kv = (rms_norm(pr['d_ckv'], mla_kv_norm) @ w_ukv).reshape(b, t, N_HEADS, MLA_NOPE + MLA_V)
    kn, dv = kv[..., :MLA_NOPE], kv[..., MLA_NOPE:]
    kr = apply_rope(pr['d_kr'][:, :, None, :], *rot_mla)[:, :, 0]
    o_d = mla_attention(qn, qr, kn, kr, dv)

    mkv = (mem @ w_mem_kv).reshape(b, mem.shape[1], 2, N_HEADS, HEAD_DIM)
    o_e = memory_attention(heads(pr['e_q'], N_HEADS, HEAD_DIM), mkv[:, :, 0], mkv[:, :, 1])

    o = jnp.stack([o_a, o_b, o_c, o_d, o_e], axis=2).reshape(b, t, N_BRANCH, BRANCH_W)
    y = o * jax.nn.silu(pr['z'].reshape(b, t, N_BRANCH, BRANCH_W))
    u = jnp.einsum('btnc,ncd->btnd', y, w_branch)
    g = jax.nn.sigmoid(pr['g'].reshape(b, t, N_BRANCH, d))
    out = jnp.sum(g * u, axis=2) @ w_out
    return layer_norm(DN_ALPHA * x + out, ln_g, ln_b)

def setup_inputs(seed: int = 0) -> dict:
    key = jax.random.key(seed)
    ks = jax.random.split(key, 16)
    f32 = jnp.float32

    def nrm(k, shape, scale):
        return jax.random.normal(k, shape, f32) * scale

    return {
        "x": nrm(ks[0], (BATCH, SEQ, D_MODEL), 1.0),
        "mem": nrm(ks[1], (BATCH, N_MEM, D_MODEL), 1.0),
        "ln0_g": 1.0 + nrm(ks[2], (D_MODEL,), 0.02),
        "ln0_b": nrm(ks[3], (D_MODEL,), 0.02),
        "w_in": nrm(ks[4], (DEPTH, D_MODEL, IN_WIDTH), D_MODEL ** -0.5),
        "mla_q_norm": 1.0 + nrm(ks[5], (DEPTH, Q_LORA), 0.02),
        "w_uq": nrm(ks[6], (DEPTH, Q_LORA, N_HEADS * (MLA_NOPE + MLA_ROPE)), Q_LORA ** -0.5),
        "mla_kv_norm": 1.0 + nrm(ks[7], (DEPTH, KV_LORA), 0.02),
        "w_ukv": nrm(ks[8], (DEPTH, KV_LORA, N_HEADS * (MLA_NOPE + MLA_V)), KV_LORA ** -0.5),
        "diff_lam": nrm(ks[9], (DEPTH, 4, DIFF_DIM), 0.1),
        "diff_norm": 1.0 + nrm(ks[10], (DEPTH, 2 * DIFF_DIM), 0.02),
        "w_mem_kv": nrm(ks[11], (DEPTH, D_MODEL, 2 * BRANCH_W), D_MODEL ** -0.5),
        "w_branch": nrm(ks[12], (DEPTH, N_BRANCH, BRANCH_W, D_MODEL), BRANCH_W ** -0.5 * DN_BETA),
        "w_out": nrm(ks[13], (DEPTH, D_MODEL, D_MODEL), D_MODEL ** -0.5 * DN_BETA),
        "ln_g": 1.0 + nrm(ks[14], (DEPTH, D_MODEL), 0.02),
        "ln_b": nrm(ks[15], (DEPTH, D_MODEL), 0.02),
    }

def reference(x, mem, ln0_g, ln0_b, w_in, mla_q_norm, w_uq, mla_kv_norm, w_ukv, diff_lam,
              diff_norm, w_mem_kv, w_branch, w_out, ln_g, ln_b):
    t = x.shape[1]
    rot64 = rope_tables(t, ROT_64)
    rot32 = rope_tables(t, ROT_32)
    rot_mla = rope_tables(t, MLA_ROPE)
    h = layer_norm(x, ln0_g, ln0_b)
    for l in range(DEPTH):
        h = hybrid_layer(h, mem, rot64, rot32, rot_mla, l, w_in[l], mla_q_norm[l], w_uq[l],
                         mla_kv_norm[l], w_ukv[l], diff_lam[l], diff_norm[l], w_mem_kv[l],
                         w_branch[l], w_out[l], ln_g[l], ln_b[l])
    return h


_drawn_inputs = setup_inputs


def setup_inputs(seed=0):
    import zlib

    import numpy as np

    out = dict(_drawn_inputs(seed))
    spreads = {}
    factors = {'mem': 7.104,
     'ln0_g': 2.775,
     'ln0_b': 2.668,
     'mla_q_norm': 8.0,
     'w_uq': 5.112,
     'mla_kv_norm': 8.0,
     'w_ukv': 3.924,
     'diff_lam': 8.0,
     'diff_norm': 8.0,
     'w_mem_kv': 6.735}
    for name, (base, spread) in spreads.items():
        noise = np.random.default_rng([zlib.crc32(name.encode()), seed]).standard_normal(out[name].shape)
        drawn = base * np.exp(spread * noise) if base else spread * noise
        out[name] = __import__('jax').numpy.asarray(drawn.astype(out[name].dtype))
    for name, factor in factors.items():
        out[name] = (out[name] * factor).astype(out[name].dtype)
    return out
```

```python
from contextlib import ExitStack

import numpy as np

import concourse.bass as bass
from concourse import mybir

F32 = mybir.dt.float32
F32R = mybir.dt.float32r
ALU = mybir.AluOpType
ACT = mybir.ActivationFunctionType
AX = mybir.AxisListType

P = 128
D = 1024
T = 512
DEPTH = 2
NT = T // P
KD = D // P
MEM = 256
NH = 4
HD = 64
BW = NH * HD
N_BRANCH = 5
IH, ID = 8, 32
TOPK = min(256, T // 4)
ROUNDS = TOPK // 8
QL, KVL = 256, 128
MR = 32
ROPE_THETA = 500000.0
ALPHA = (2 * DEPTH) ** 0.25
LN_EPS = 1e-5
RMS_EPS = 1e-6
MASKED = -1.0e30
TAKEN = -3.0e38

NAMES = [("a_q", BW), ("a_k", BW), ("a_v", BW), ("i_q", IH * ID), ("i_k", ID), ("i_w", IH),
         ("b_q", BW), ("b_k", BW), ("b_v", BW), ("c_q", BW), ("c_k", BW), ("c_v", BW),
         ("d_cq", QL), ("d_ckv", KVL), ("d_kr", MR), ("e_q", BW), ("z", N_BRANCH * BW), ("g", N_BRANCH * D)]
OFF = {}
_at = 0
for _n, _w in NAMES:
    OFF[_n] = _at
    _at += _w
IN_WIDTH = _at

BRANCH = {b: i for i, b in enumerate("ABCDE")}
SCALE = {"A": HD ** -0.5, "B": HD ** -0.5, "C": (HD // 2) ** -0.5, "D": (HD + MR) ** -0.5, "E": HD ** -0.5}
UNITS = {"A": 16, "B": 16, "C": 32, "D": 16, "E": 16}

CHUNKS = {
    "E": [(OFF["e_q"], BW), (OFF["z"] + 4 * BW, BW)],
    "IX": [(OFF["i_q"], IH * ID + ID + IH)],
    "A1": [(OFF["a_v"], BW), (OFF["z"], BW)], "A0": [(OFF["a_q"], 2 * BW)],
    "B1": [(OFF["b_v"], BW), (OFF["z"] + BW, BW)], "B0": [(OFF["b_q"], 2 * BW)],
    "C1": [(OFF["c_v"], BW), (OFF["z"] + 2 * BW, BW)], "C0": [(OFF["c_q"], 2 * BW)],
    "D0": [(OFF["d_cq"], QL + KVL + MR)], "D1": [(OFF["z"] + 3 * BW, BW)],
}
for _b in "ABCDE":
    for _c in range(2):
        CHUNKS[f"g{_b}{_c}"] = [(OFF["g"] + BRANCH[_b] * D + _c * 512, 512)]
WIDTH = {c: sum(w for _, w in r) for c, r in CHUNKS.items()}
WIDTH["O0"] = WIDTH["O1"] = 512
ORDER = ["IX", "E", "A1", "A0", "B1", "B0", "gE0", "gE1", "gB0", "gB1", "C0", "C1", "D0", "D1",
         "gA0", "gA1", "gC0", "gC1", "gD0", "gD1", "O0", "O1"]


LAG_T, LAG_V = 2, 3


def att_steps(b):
    n = UNITS[b]
    out = []
    for i in range(n + LAG_V + (3 if b == "C" else 0)):
        first = [("S", b, i)] if i < n else []
        if 0 <= i - LAG_V < n:
            first.insert(0, ("V", b, i - LAG_V))
        second = [("T", b, i - LAG_T)] if 0 <= i - LAG_T < n else []
        if b == "C":
            for lag, kind in ((1, "R"), (3, "F")):
                t, j = divmod(i - LAG_V - lag, 8)
                if j == 7 and 0 <= t < NT:
                    second.append((kind, t))
        out += [[x for x in first if x[0] == "V"] + second, [x for x in first if x[0] == "S"]]
    return out


def plan():
    groups = [(c, kh, t, part) for c in ORDER for kh in range(2) for t in range(NT) for part in range(2)]
    at = {g: i for i, g in enumerate(groups)}
    extra = [[] for _ in groups]

    def spread(steps, first, last):
        a, b = at[first + (0,)], at[last + (1,)]
        for i, s in enumerate(steps):
            extra[a + (i * (b - a + 1)) // len(steps)].extend(s)

    halves = [(c, kh) for c in ORDER for kh in range(2)]
    for i in range(1, len(halves)):
        c, kh = halves[i - 1]
        extra[at[(c, kh, 0, 0)]].append(("split",) + halves[i])
        if c[0] == "g" and kh == 0:
            extra[at[(c, 0, 1, 0)]].append(("splitb", c))
    start = [("mkv",), ("split", ORDER[0], 0), ("xj", 0, 0), ("xj", 0, 1), ("xj", 1, 0), ("xj", 1, 1)]
    extra[at[(ORDER[0], 0, 0, 1)]] += [("xj", 2, 0), ("xj", 2, 1)]
    extra[at[(ORDER[0], 0, 1, 1)]] += [("xj", 3, 0), ("xj", 3, 1)]

    def tiles(*kind):
        return [[kind + (t,)] for t in range(NT)]

    spread(tiles("ixj"), ("IX", 1, 3), ("E", 0, 1))
    idx = [[("I", t, h)] for t in range(1, NT) for h in range(IH)]
    spread(idx, ("E", 0, 2), ("A1", 1, 3))
    rounds = [[("K", t, r)] for t in range(1, NT) for r in range(ROUNDS)] + [[("KB",)]]
    spread(rounds[:ROUNDS], ("A1", 0, 0), ("A0", 0, 0))
    spread(rounds[ROUNDS:2 * ROUNDS], ("A0", 0, 1), ("B1", 1, 3))
    spread(rounds[2 * ROUNDS:], ("B0", 0, 0), ("gE1", 1, 2))
    spread(tiles("ej"), ("E", 1, 2), ("A1", 0, 0))
    spread(att_steps("E"), ("A1", 0, 1), ("A0", 1, 3))
    spread(tiles("qk", "A"), ("B1", 0, 0), ("B1", 0, 1))
    spread(tiles("yj", "E"), ("B1", 0, 2), ("B1", 0, 3))
    spread(tiles("qk", "B"), ("B0", 1, 2), ("gE0", 0, 1))
    spread(att_steps("B"), ("gE0", 0, 2), ("gE1", 1, 3))
    spread(tiles("yj", "B"), ("gB0", 0, 0), ("gB0", 0, 3))
    spread(att_steps("A"), ("gB0", 0, 1), ("gB1", 1, 3))
    spread(tiles("yj", "A"), ("C0", 0, 0), ("C0", 0, 3))
    spread(tiles("qk", "C"), ("C0", 1, 2), ("C1", 0, 1))
    spread(att_steps("C"), ("C1", 1, 1), ("gA1", 0, 3))
    spread([[("rms", t)] for t in range(NT)], ("D0", 1, 1), ("D1", 0, 0))
    spread(tiles("cj"), ("D1", 0, 1), ("gA0", 0, 0))
    spread([[("du", 0), ("du", 1)], [("dj", 0), ("du", 2)], [("dj", 1), ("du", 3)], [("dj", 2)], [("dj", 3)]],
           ("gA1", 1, 0), ("gC0", 0, 0))
    spread(tiles("yj", "C"), ("gC0", 0, 0), ("gC0", 0, 3))
    spread(att_steps("D"), ("gC0", 0, 1), ("gC1", 1, 3))
    spread(tiles("yj", "D"), ("gD0", 0, 0), ("gD0", 0, 3))
    spread([[("mj", t, 0), ("mj", t, 1)] for t in range(2)], ("gD1", 1, 2), ("gD1", 1, 3))
    extra[at[("O0", 0, 0, 1)]] += [("mj", 2, 0), ("mj", 2, 1)]
    extra[at[("O0", 0, 1, 1)]] += [("mj", 3, 0), ("mj", 3, 1)]
    extra[at[("O1", 1, 1, 1)]] += [("l1", 0)]
    extra[at[("O1", 1, 2, 1)]] += [("l1", 1), ("l2", 0)]
    extra[at[("O1", 1, 3, 1)]] += [("l1", 2), ("l2", 1), ("l1", 3), ("l2", 2), ("l2", 3)]
    steps = list(start)
    for g, more in zip(groups, extra):
        steps.append(("grp",) + g)
        steps += more
    return steps


PLAN = plan()
SPLITS = [(c, kh) for c in ORDER for kh in range(2)]


def loads():
    out = [("mk", 0), ("mk", 1), ("prm", 0)]
    for c in ORDER:
        out.append((c, 0))
        out.append((c, 1))
        if c[0] == "g":
            out.append(("wb", c))
        if c == "gA1":
            out.append(("du", 0))
    return out


LOADS = loads()
NRAW, NW = 2, 2
assert len(LOADS) % NRAW == 0 and len(SPLITS) % NW == 0

C_MASK, C_ID = 0, T
C_ROPE = C_ID + P
R64, R32, RM = 0, 32, 48
ROPE_W = 48 + 2 * MR
C_LAM = C_ROPE + NT * ROPE_W
C_EPS = C_LAM + 2 * DEPTH
C_RE = C_EPS + 2
C_N = C_RE + 1


def constants():
    c = np.zeros((P, C_N), np.float32)
    p = np.arange(P)
    c[:, C_MASK + T - P:C_MASK + T] = np.where(p[None, :] <= p[:, None], 0.0, MASKED)
    c[:, C_ID:C_ID + P] = np.eye(P)
    for t in range(NT):
        pos = (t * P + p).astype(np.float32)
        for off, rot in ((R64, 16), (R32, 8), (RM, MR)):
            inv = np.float32(ROPE_THETA) ** (-np.arange(0, rot, 2, dtype=np.float32) / np.float32(rot))
            ang = pos[:, None] * inv[None, :].astype(np.float32)
            co, si = np.cos(ang), np.sin(ang)
            at = C_ROPE + t * ROPE_W + off
            c[:, at:at + 2 * rot] = np.concatenate([co, co, -si, si], 1)
    for layer in range(DEPTH):
        init = 0.8 - 0.6 * float(np.exp(-0.3 * layer))
        c[:, C_LAM + layer] = -init
        c[:, C_LAM + DEPTH + layer] = (1.0 - init) * 0.5
    c[:, C_EPS] = LN_EPS
    c[:, C_EPS + 1] = LN_EPS / ALPHA ** 2
    c[:, C_RE] = RMS_EPS
    return c


class Tally:

    def __init__(self, sem, known):
        self.sem, self.n, self.base, self.known = sem, 0, 0, known

    def step(self, key, by=1):
        self.n += by
        self.known.setdefault(key, self.n - self.base if key[0] != "first" else self.n)
        return by

    def layer(self, layer):
        if layer == 1:
            self.known.setdefault("per_layer", self.n - self.base)
        if layer == 0:
            self.known["ahead"] = self.n
        self.base = self.n

    def at(self, layer, key):
        if key[0] == "first":
            return self.known.get(key, 1)
        return self.known.get("ahead", 0) + layer * self.known.get("per_layer", 0) + self.known.get(key, 1)


def build(nc, known, x, mem, ln0_g, ln0_b, w_in, mla_q_norm, w_uq, mla_kv_norm, w_ukv, diff_lam,
          diff_norm, w_mem_kv, w_branch, w_out, ln_g, ln_b, consts, out):
    with ExitStack() as ctx:
        def sb(name, shape, dt=F32):
            return ctx.enter_context(nc.sbuf_tensor(name, shape, dt))

        def tally(name):
            return Tally(ctx.enter_context(nc.semaphore(name)), known.setdefault(name, {}))

        X = sb("residual", [P, NT, D])
        XTH = sb("stationary_head", [P, KD, T], F32R)
        XTL = sb("stationary_rest", [P, KD, T], F32R)
        RAW = sb("raw_weights", [P, NRAW, 4 * 512])
        WH = sb("weights_head", [P, NW, 4 * 512], F32R)
        WL = sb("weights_rest", [P, NW, 4 * 512], F32R)
        WBH = sb("branch_weights_head", [P, 2, 512], F32R)
        WBL = sb("branch_weights_rest", [P, 2, 512], F32R)
        ST = sb("staged_features", [P, NT, 512])
        VZ = sb("values_and_gates", [P, 2, NT, 512])
        KC = sb("mla_keys", [P, 2, NH, HD + MR])
        QK = sb("queries_keys_T", [P, 4, T])
        QK2 = sb("queries_keys_T2", [P, 4, T])
        M = sb("merged", [P, NT, D])
        YTH = sb("branch_out_T_head", [P, 2, T], F32R)
        YTL = sb("branch_out_T_rest", [P, 2, T], F32R)
        SM = sb("probabilities", [P, 2, T])
        PT = sb("probabilities_T", [P, T])
        TH = sb("activated", [P, 2, 512])
        SC_W = [0, 0, 2 * P, 5 * P]
        SC = sb("index_scores", [P, 9 * P])
        IW = sb("index_weights", [P, NT, IH])
        LN_IN = VZ[:, 0, :, :].rearrange("p t n -> p (t n)")
        MEM_IN = VZ[:, 1, :, :].rearrange("p t n -> p (t n)").rearrange("p (t d) -> p t d", t=2)
        MEMT = sb("memory_T", [P, KD, MEM])
        MKT = sb("memory_keys_T", [P, 2, MEM])
        MV = sb("memory_values", [P, 2, BW])
        PRM_N = QL + KVL + HD + 4 * ID
        PRM = sb("layer_norms", [P, PRM_N])
        CN = sb("consts_sb", [P, C_N])
        JNK = KC[:].rearrange("p a h c -> p (a h c)")[:, 0:QL]
        DS = sb("vector_scratch", [P, 512])
        DF = sb("diff_out", [P, BW])
        NMX = sb("max_of_scores", [P, 4])
        RS = sb("row_sums", [P, 2, 8])
        RI = sb("reciprocals", [P, 8])
        SS = sb("norm_sums", [P, 16])
        MS = sb("mla_norm_sums", [P, NT, 4])
        BN = sb("norm_stats", [P, 16])
        LAM = sb("lambdas", [P, 8])
        DN = sb("diff_norm_scaled", [P, HD])
        TOP = sb("top_eight", [P, 8])

        G = [ctx.enter_context(nc.psum_tensor(f"product{i}", [P, 512], F32)) for i in range(NT)]
        U = ctx.enter_context(nc.psum_tensor("branch_product", [P, 512], F32))
        S = ctx.enter_context(nc.psum_tensor("scores", [P, 512], F32))
        TP = ctx.enter_context(nc.psum_tensor("transposed", [P, 512], F32))
        O = ctx.enter_context(nc.psum_tensor("context", [P, 512], F32))

        raw = [tally(f"raw_loaded{i}") for i in range(NRAW)]
        first_in = tally("consts_loaded")
        x_in = [tally(f"x_loaded{t}") for t in range(NT)]
        mem_in = tally("memory_loaded")
        first_ln_in = tally("first_norm_loaded")
        ln_in = tally("layer_norm_loaded")
        stored = tally("stored")
        gemm = tally("product_done")
        u_done = tally("branch_product_done")
        s_done = tally("scores_done")
        t_done = tally("transposes_done")
        v_done = tally("context_done")
        m_done = tally("small_products_done")
        head = tally("head_split")
        act_out = tally("activated_ready")
        copied = tally("product_copied")
        exped = tally("probabilities_ready")
        moved = tally("transposed_moved")
        rooted = tally("root_ready")
        scaled = tally("residual_scaled")
        a_chain = tally("scalar_step")
        masked = tally("scores_masked")
        used = tally("activated_used")
        gated = tally("gates_ready")
        roped = tally("rotated")
        final = tally("branch_tile_ready")
        rest = tally("rest_of_stationary")
        summed = tally("squares_summed")
        residual = tally("residual_added")
        v_chain = tally("vector_step")
        gained = tally("gain_applied")
        lo_done = tally("rest_split")
        normed = tally("normed")
        prm_copied = tally("norms_copied")

        every = [*raw, prm_copied, first_in, *x_in, mem_in, first_ln_in, ln_in, stored, gemm, u_done, s_done, t_done, v_done, m_done, head,
                 act_out, copied, exped, moved, rooted, a_chain, masked, used, gated, roped, final, rest,
                 summed, residual, normed, scaled, gained, v_chain, lo_done]

        def new_layer(mine, layer):
            for c in mine:
                c.layer(layer)

        ident = CN[:, C_ID:C_ID + P]

        def mask(w):
            return CN[:, C_MASK + T - w:C_MASK + T]

        def rope(t, off, half):
            at = C_ROPE + t * ROPE_W + off
            return CN[:, at:at + 2 * half], CN[:, at + 2 * half:at + 3 * half], CN[:, at + 3 * half:at + 4 * half]

        def raw_slot(item):
            return LOADS.index(item) % NRAW

        def w_slot(c, kh):
            return SPLITS.index((c, kh)) % NW

        def half_view(buf, slot, c):
            w = WIDTH[c]
            return buf[:, slot, 0:4 * w].rearrange("p (k n) -> p k n", k=4)

        def unit(b, u):
            per = 8 if b == "C" else 4
            t, j = u // per, u % per
            return t, j, MEM if b == "E" else (t + 1) * P

        def vz(b):
            return 0 if b in "AC" else 1

        def before(key_step):
            same = [s for s in PLAN if s[0] == key_step[0]]
            i = same.index(key_step)
            return same[i - 1] if i else None

        block = ctx.enter_context(nc.Block())

        @block.sync
        def _(sp):
            sp.dma_start(CN[:], consts).then_inc(first_in.sem, first_in.step(("first", "c"), 16))
            sp.dma_start(MEM_IN, mem[0].rearrange("(t p) d -> p t d", p=P)).then_inc(mem_in.sem, mem_in.step(("first", "m"), 16))
            for L in range(DEPTH):
                new_layer([*raw, ln_in], L)
                for i, item in enumerate(LOADS):
                    s = i % NRAW
                    if i >= NRAW:
                        old, Lo = LOADS[i - NRAW], L
                    elif L > 0:
                        old, Lo = LOADS[len(LOADS) - NRAW + i], L - 1
                    else:
                        old, Lo = None, 0
                    if old is None:
                        pass
                    elif old[0] == "mk":
                        sp.wait_ge(m_done.sem, m_done.at(Lo, ("mkv", old[1])))
                    elif old[0] == "du":
                        sp.wait_ge(m_done.sem, m_done.at(Lo, ("du", NT - 1)))
                    elif old[0] == "prm":
                        sp.wait_ge(prm_copied.sem, prm_copied.at(Lo, ("prm",)))
                    else:
                        sp.wait_ge(lo_done.sem, lo_done.at(Lo, old))
                    if item == ("gD1", 0):
                        sp.wait_ge(t_done.sem, t_done.at(L, ("yj", "C", NT - 1)))
                        sp.dma_start(LN_IN[:, 0:D], ln_g[L].partition_broadcast(P)).then_inc(ln_in.sem, ln_in.step(("half",), 16))
                        sp.dma_start(LN_IN[:, D:2 * D], ln_b[L].partition_broadcast(P)).then_inc(ln_in.sem, ln_in.step(("ln",), 16))
                    sem = raw[s]
                    if item[0] == "mk":
                        sp.dma_start(RAW[:, s, :].rearrange("p (k n) -> p k n", k=4),
                                     w_mem_kv[L, item[1] * 512:(item[1] + 1) * 512, :].rearrange("(k p) n -> p k n", p=P)).then_inc(sem.sem, sem.step(item, 16))
                    elif item[0] == "wb":
                        b, c = BRANCH[item[1][1]], int(item[1][2])
                        sp.dma_start(RAW[:, s, 0:1024].rearrange("p (k n) -> p k n", k=2),
                                     w_branch[L, b, :, c * 512:(c + 1) * 512].rearrange("(k p) n -> p k n", p=P)).then_inc(sem.sem, sem.step(item, 16))
                    elif item[0] == "du":
                        sp.dma_start(RAW[:, s, 0:768].rearrange("p (k n) -> p k n", k=2),
                                     w_uq[L].rearrange("(k p) n -> p k n", p=P)).then_inc(sem.sem, sem.step(("half", "du"), 16))
                        sp.dma_start(RAW[:, s, 768:1280], w_ukv[L]).then_inc(sem.sem, sem.step(item, 16))
                    elif item[0] == "prm":
                        at = 0
                        for src, w in ((mla_q_norm[L], QL), (mla_kv_norm[L], KVL), (diff_norm[L], HD),
                                       (diff_lam[L].rearrange("a b -> (a b)"), 4 * ID)):
                            key = item if at + w == PRM_N else ("part", "prm", at)
                            sp.dma_start(RAW[:, s, at:at + w], src.partition_broadcast(P)).then_inc(sem.sem, sem.step(key, 16))
                            at += w
                    elif item[0][0] == "O":
                        c, kh = int(item[0][1]), item[1]
                        sp.dma_start(RAW[:, s, :].rearrange("p (k n) -> p k n", k=4),
                                     w_out[L, kh * 512:(kh + 1) * 512, c * 512:(c + 1) * 512].rearrange("(k p) n -> p k n", p=P)).then_inc(sem.sem, sem.step(item, 16))
                    else:
                        c, kh = item
                        view = half_view(RAW, s, c)
                        at, ranges = 0, CHUNKS[c]
                        for j, (c0, w) in enumerate(ranges):
                            key = item if j == len(ranges) - 1 else ("part", c, kh)
                            sp.dma_start(view[:, :, at:at + w],
                                         w_in[L, kh * 512:(kh + 1) * 512, c0:c0 + w].rearrange("(k p) n -> p k n", p=P)).then_inc(sem.sem, sem.step(key, 16))
                            at += w
            for t in range(NT):
                sp.wait_ge(normed.sem, normed.at(DEPTH - 1, ("t", t)))
                sp.dma_start(out[0, t * P:(t + 1) * P, :], X[:, t, :]).then_inc(stored.sem, stored.step(("first", t), 16))
            sp.wait_ge(stored.sem, stored.at(0, ("first", NT - 1)))

        @block.gpsimd
        def _(pool):
            def offset(L, t, key, b):
                pool.wait_ge(gained.sem, gained.at(L, key))
                nc.gpsimd.tensor_tensor(X[:, t, :], X[:, t, :], b, ALU.add).then_inc(normed.sem, normed.step(key))

            for t in range(NT):
                offset(0, t, ("first", t), LN_IN[:, D:2 * D])
            for L in range(DEPTH):
                new_layer([lo_done, normed, prm_copied], L)
                if L > 0:
                    pool.wait_ge(final.sem, final.at(L - 1, ("D", NT - 1)))
                rw = raw[raw_slot(("prm", 0))]
                pool.wait_ge(rw.sem, rw.at(L, ("prm", 0)))
                nc.gpsimd.tensor_copy(PRM[:], RAW[:, raw_slot(("prm", 0)), 0:PRM_N]).then_inc(prm_copied.sem, prm_copied.step(("prm",)))
                for step in PLAN:
                    if step[0] == "l2":
                        offset(L, step[1], ("t", step[1]), LN_IN[:, D:2 * D])
                    if step[0] == "split":
                        item = step[1:]
                        pool.wait_ge(head.sem, head.at(L, item))
                        sw, sr, n = w_slot(*item), raw_slot(item), 4 * WIDTH[item[0]]
                        nc.gpsimd.tensor_tensor(WL[:, sw, 0:n], RAW[:, sr, 0:n], WH[:, sw, 0:n].bitcast(F32),
                                                ALU.subtract).then_inc(lo_done.sem, lo_done.step(item))
                    elif step[0] == "splitb":
                        item = ("wb", step[1])
                        pool.wait_ge(head.sem, head.at(L, item))
                        sr = raw_slot(item)
                        nc.gpsimd.tensor_tensor(WBL[:].rearrange("p k n -> p (k n)"), RAW[:, sr, 0:1024],
                                                WBH[:].rearrange("p k n -> p (k n)").bitcast(F32),
                                                ALU.subtract).then_inc(lo_done.sem, lo_done.step(item))

        @block.tensor
        def _(pe):
            freed = {}

            def claim(bank):
                if bank in freed:
                    c, L, key = freed.pop(bank)
                    pe.wait_ge(c.sem, c.at(L, key))

            def product3(dst, xh, xl, wh, wl, start, stop):
                nc.tensor.matmul(dst, xh, wh, start=start, stop=False)
                nc.tensor.matmul(dst, xh, wl, start=False, stop=False)
                return nc.tensor.matmul(dst, xl, wh, start=False, stop=stop)

            pe.wait_ge(first_in.sem, first_in.at(0, ("first", "c")))
            pe.wait_ge(mem_in.sem, mem_in.at(0, ("first", "m")))
            for j in range(4):
                for i in range(4):
                    k, t = 2 * j + i // 2, i % 2
                    last = nc.tensor.transpose(G[j][:, i * P:(i + 1) * P], MEM_IN[:, t, k * P:(k + 1) * P], ident)
                last.then_inc(t_done.sem, t_done.step(("first", "mem", j)))
                freed[f"G{j}"] = (moved, 0, ("first", j))
            for L in range(DEPTH):
                new_layer([gemm, u_done, s_done, t_done, v_done, m_done], L)
                for step in PLAN:
                    kind = step[0]
                    if kind == "grp":
                        _, c, kh, t, part = step
                        w = WIDTH[c]
                        if kh == 0 and part == 0:
                            claim(f"G{t}")
                        if c == ORDER[0] and kh == 0:
                            pe.wait_ge(rest.sem, rest.at(L, ("x", t, 1)))
                        if c[0] == "O" and kh == 0:
                            pe.wait_ge(rest.sem, rest.at(L, ("m", t, 1)))
                        if t == 0 and part == 0:
                            pe.wait_ge(lo_done.sem, lo_done.at(L, (c, kh)))
                        wh, wl = (half_view(b, w_slot(c, kh), c) for b in (WH, WL))
                        for k in range(2 * part, 2 * part + 2):
                            kk = 4 * kh + k
                            last = product3(G[t][:, 0:w], XTH[:, kk, t * P:(t + 1) * P], XTL[:, kk, t * P:(t + 1) * P],
                                            wh[:, k, :], wl[:, k, :], kk == 0, kk == KD - 1)
                        if part == 0:
                            continue
                        last.then_inc(gemm.sem, gemm.step((c, kh, t)))
                        if kh == 1:
                            if c in ("A0", "B0", "C0", "IX"):
                                freed[f"G{t}"] = (copied, L, (c, t))
                            elif c[0] == "g":
                                freed[f"G{t}"] = (act_out, L, (c, t))
                            elif c[0] == "O":
                                freed[f"G{t}"] = (residual, L, (c, t))
                            elif c == "D0":
                                freed[f"G{t}"] = (gated, L, (c, t))
                            else:
                                freed[f"G{t}"] = (used, L, (c, t))
                            if c[0] == "g":
                                claim("U")
                                if t == 0:
                                    pe.wait_ge(lo_done.sem, lo_done.at(L, ("wb", c)))
                                    pe.wait_ge(rest.sem, rest.at(L, ("y", c[1], NT - 1)))
                                for k in range(2):
                                    last = product3(U[:], YTH[:, k, t * P:(t + 1) * P], YTL[:, k, t * P:(t + 1) * P],
                                                    WBH[:, k, :], WBL[:, k, :], k == 0, k == 1)
                                last.then_inc(u_done.sem, u_done.step((c, t)))
                                freed["U"] = (used, L, (c, t))
                    elif kind == "mkv":
                        for t in range(4):
                            claim(f"G{t}")
                        if L == 0:
                            for j in range(4):
                                pe.wait_ge(moved.sem, moved.at(0, ("first", j)))
                        for kh in range(2):
                            rw = raw[raw_slot(("mk", kh))]
                            pe.wait_ge(rw.sem, rw.at(L, ("mk", kh)))
                            wv = RAW[:, raw_slot(("mk", kh)), :].rearrange("p (k n) -> p k n", k=4)
                            for k in range(4):
                                kk = 4 * kh + k
                                for j in range(2):
                                    nc.tensor.matmul(G[j][:, 0:MEM], wv[:, k, j * P:(j + 1) * P], MEMT[:, kk, :],
                                                     start=kk == 0, stop=kk == KD - 1)
                                for j in range(2):
                                    last = nc.tensor.matmul(G[2 + j][:, 0:BW], MEMT[:, kk, j * P:(j + 1) * P],
                                                            wv[:, k, BW:2 * BW], start=kk == 0, stop=kk == KD - 1)
                            last.then_inc(m_done.sem, m_done.step(("mkv", kh)))
                        for t in range(4):
                            freed[f"G{t}"] = (copied, L, ("mkv", t))
                    elif kind in ("xj", "mj"):
                        _, t, j = step
                        name, bank = ("TP", TP) if j == 0 else ("O", O)
                        claim(name)
                        if kind == "xj":
                            if L == 0:
                                pe.wait_ge(normed.sem, normed.at(0, ("first", t)))
                            else:
                                pe.wait_ge(normed.sem, normed.at(L - 1, ("t", t)))
                            src = X
                        else:
                            pe.wait_ge(used.sem, used.at(L, ("gD1", t)))
                            src = M
                        for i in range(4):
                            k = 4 * j + i
                            last = nc.tensor.transpose(bank[:, i * P:(i + 1) * P], src[:, t, k * P:(k + 1) * P], ident)
                        last.then_inc(t_done.sem, t_done.step(step))
                        freed[name] = (rest, L, (kind[0], t, j))
                    elif kind == "yj":
                        _, b, t = step
                        claim("TP")
                        pe.wait_ge(final.sem, final.at(L, (b, t)))
                        for i in range(2):
                            last = nc.tensor.transpose(TP[:, i * P:(i + 1) * P], VZ[:, vz(b), t, BW + i * P:BW + (i + 1) * P], ident)
                        last.then_inc(t_done.sem, t_done.step(step))
                        freed["TP"] = (rest, L, ("y", b, t))
                    elif kind in ("ej", "ixj", "qk", "cj", "dj"):
                        t = step[-1]
                        claim("TP")
                        if kind == "ej":
                            pe.wait_ge(copied.sem, copied.at(L, ("E", t)))
                            src, n, w = VZ[:, 1, t, :], 2, P
                        elif kind == "ixj":
                            pe.wait_ge(roped.sem, roped.at(L, ("IX", t)))
                            src, n, w = ST[:, t, :], 3, P
                        elif kind == "qk":
                            pe.wait_ge(roped.sem, roped.at(L, (step[1] + "0", t)))
                            src, n, w = ST[:, t, :], 4, P
                        elif kind == "cj":
                            pe.wait_ge(gated.sem, gated.at(L, ("D0", t)))
                            src, n, w = ST[:, t, :], 3, P
                        else:
                            pe.wait_ge(roped.sem, roped.at(L, ("dq", t)))
                            src, n, w = ST[:, t, :], NH, HD + MR
                        for i in range(n):
                            last = nc.tensor.transpose(TP[0:w, i * P:(i + 1) * P], src[:, i * w:(i + 1) * w], ident)
                        last.then_inc(t_done.sem, t_done.step(step))
                        freed["TP"] = (moved, L, step)
                        if kind == "dj":
                            claim("O")
                            for i in range(n):
                                last = nc.tensor.transpose(O[0:w, i * P:(i + 1) * P], KC[:, t % 2, i, :], ident)
                            last.then_inc(t_done.sem, t_done.step(("dk", t)))
                            freed["O"] = (moved, L, ("dk", t))
                    elif kind == "du":
                        t = step[1]
                        claim("O")
                        claim("TP")
                        if t == 0:
                            rw = raw[raw_slot(("du", 0))]
                            pe.wait_ge(rw.sem, rw.at(L, ("du", 0)))
                        pe.wait_ge(moved.sem, moved.at(L, ("cj", t)))
                        wv = RAW[:, raw_slot(("du", 0)), :]
                        for k in range(2):
                            nc.tensor.matmul(O[:, 0:384], QK2[:, k, t * P:(t + 1) * P], wv[:, k * 384:(k + 1) * 384],
                                             start=k == 0, stop=k == 1)
                        nc.tensor.matmul(TP[:], QK2[:, 2, t * P:(t + 1) * P], wv[:, 768:1280],
                                         start=True, stop=True).then_inc(m_done.sem, m_done.step(step))
                        freed["O"] = (copied, L, ("dq", t))
                        freed["TP"] = (copied, L, ("dk", t))
                    elif kind == "I":
                        _, t, h = step
                        claim("U")
                        if h == 0:
                            pe.wait_ge(moved.sem, moved.at(L, ("ixj", t)))
                        w, r = (t + 1) * P, slice(32 * (h % 4), 32 * (h % 4) + 32)
                        nc.tensor.matmul(U[:, 0:w], QK2[r, 2 + h // 4, t * P:(t + 1) * P], QK[r, 0, 0:w],
                                         start=True, stop=True, tile_position=(32 * (h % 4), 0)).then_inc(s_done.sem, s_done.step(step))
                        freed["U"] = (act_out, L, step)
                    elif kind == "S":
                        _, b, u = step
                        t, j, w = unit(b, u)
                        claim("S")
                        if j == 0:
                            need = {"E": ("ej", t), "D": ("dk", t)}.get(b, ("qk", b, t))
                            pe.wait_ge(moved.sem, moved.at(L, need))
                            if b == "E" and u == 0:
                                pe.wait_ge(copied.sem, copied.at(L, ("mkv", 3)))
                        q = slice(t * P, (t + 1) * P)
                        if b == "E":
                            r = slice(64 * (j % 2), 64 * (j % 2) + 64)
                            lhs, rhs, row = QK2[r, j // 2, q], MKT[r, j // 2, :], r.start
                        elif b == "D":
                            lhs, rhs, row = QK[0:HD + MR, j, q], QK2[0:HD + MR, j, 0:w], 0
                        elif b == "C":
                            r = slice(32 * (j % 4), 32 * (j % 4) + 32)
                            lhs, rhs, row = QK[r, j // 4, q], QK[r, 2 + j // 4, 0:w], r.start
                        else:
                            r = slice(64 * (j % 2), 64 * (j % 2) + 64)
                            qk = QK2 if b == "A" else QK
                            lhs, rhs, row = qk[r, j // 2, q], qk[r, 2 + j // 2, 0:w], r.start
                        nc.tensor.matmul(S[:, 0:w], lhs, rhs, start=True, stop=True,
                                         tile_position=(row, 0)).then_inc(s_done.sem, s_done.step(step))
                        freed["S"] = (masked, L, (b, u))
                    elif kind == "T":
                        _, b, u = step
                        t, j, w = unit(b, u)
                        claim("TP")
                        pe.wait_ge(exped.sem, exped.at(L, (b, u)))
                        for i in range(w // P):
                            last = nc.tensor.transpose(TP[:, i * P:(i + 1) * P], SM[:, u % 2, i * P:(i + 1) * P], ident)
                        last.then_inc(t_done.sem, t_done.step(step))
                        freed["TP"] = (moved, L, step)
                    elif kind == "V":
                        _, b, u = step
                        t, j, w = unit(b, u)
                        if j == 0:
                            claim("O")
                            if b == "D":
                                pe.wait_ge(copied.sem, copied.at(L, ("dk", t)))
                            elif b != "E":
                                pe.wait_ge(copied.sem, copied.at(L, (b + "1", t)))
                        pe.wait_ge(moved.sem, moved.at(L, ("T", b, u)))
                        h = j // 2 if b == "C" else j
                        for i in range(w // P):
                            v = MV[:, i, h * HD:(h + 1) * HD] if b == "E" else VZ[:, vz(b), i, h * HD:(h + 1) * HD]
                            last = nc.tensor.matmul(O[:, j * HD:(j + 1) * HD], PT[:, i * P:(i + 1) * P], v,
                                                    start=i == 0, stop=i == w // P - 1)
                        last.then_inc(v_done.sem, v_done.step((b, u)))
                        if j == (7 if b == "C" else 3):
                            freed["O"] = (summed if b == "C" else final, L, (b, t))

        @block.scalar
        def _(act):
            th_n = [0]
            th_users = []

            def th_slot(L, key):
                n = th_n[0]
                if n >= 2:
                    Lo, ko = th_users[n - 2]
                    act.wait_ge(used.sem, used.at(Lo, ko))
                th_n[0] += 1
                th_users.append((L, key))
                return n % 2

            def copy(dst, src, scale=1.0):
                return nc.scalar.activation(dst, src, ACT.Copy, scale=scale)

            def chain(ins):
                ins.then_inc(a_chain.sem, a_chain.step(("n",)))
                act.wait_ge(a_chain.sem, a_chain.n)

            def normalize(L, t, key):
                act.wait_ge(summed.sem, summed.at(L, key + ("scale",)))
                nc.scalar.activation(X[:, t, :], X[:, t, :], ACT.Identity, bias=BN[:, 4 * t + 3:4 * t + 4],
                                     scale=BN[:, 4 * t + 2:4 * t + 3]).then_inc(scaled.sem, scaled.step(key))

            for t in range(NT):
                act.dma_start(X[:, t, :], x[0, t * P:(t + 1) * P, :]).then_inc(x_in[t].sem, x_in[t].step(("first", t), 16))
                if t == 0:
                    act.dma_start(LN_IN[:, 0:D], ln0_g.partition_broadcast(P)).then_inc(first_ln_in.sem, first_ln_in.step(("first", 0), 16))
                    act.dma_start(LN_IN[:, D:2 * D], ln0_b.partition_broadcast(P)).then_inc(first_ln_in.sem, first_ln_in.step(("first", 1), 16))
            act.wait_ge(first_in.sem, first_in.at(0, ("first", "c")))
            for j in range(4):
                act.wait_ge(t_done.sem, t_done.at(0, ("first", "mem", j)))
                copy(MEMT[:, 2 * j:2 * j + 2, :], G[j][:].rearrange("p (k n) -> p k n", k=2)).then_inc(moved.sem, moved.step(("first", j)))
            for t in range(NT):
                act.wait_ge(summed.sem, summed.at(0, ("first", t)))
                nc.scalar.activation(SS[:, 12 + t:13 + t], BN[:, 4 * t + 1:4 * t + 2], ACT.Sqrt,
                                     bias=CN[:, C_EPS:C_EPS + 1]).then_inc(rooted.sem, rooted.step(("first", t)))
                normalize(0, t, ("first", t))
            for L in range(DEPTH):
                new_layer([head, act_out, copied, exped, moved, rooted, scaled, a_chain], L)
                for step in PLAN:
                    kind = step[0]
                    if kind == "split":
                        item = step[1:]
                        rw = raw[raw_slot(item)]
                        act.wait_ge(rw.sem, rw.at(L, item))
                        i = SPLITS.index(item)
                        if i >= NW:
                            act.wait_ge(gemm.sem, gemm.at(L, SPLITS[i - NW] + (NT - 1,)))
                        elif L > 0:
                            act.wait_ge(gemm.sem, gemm.at(L - 1, SPLITS[len(SPLITS) - NW + i] + (NT - 1,)))
                        n = 4 * WIDTH[item[0]]
                        copy(WH[:, i % NW, 0:n], RAW[:, raw_slot(item), 0:n]).then_inc(head.sem, head.step(item))
                    elif kind == "splitb":
                        item = ("wb", step[1])
                        rw = raw[raw_slot(item)]
                        act.wait_ge(rw.sem, rw.at(L, item))
                        prev = before(step)
                        if prev:
                            act.wait_ge(u_done.sem, u_done.at(L, (prev[1], NT - 1)))
                        elif L > 0:
                            act.wait_ge(u_done.sem, u_done.at(L - 1, ("gD1", NT - 1)))
                        copy(WBH[:].rearrange("p k n -> p (k n)"), RAW[:, raw_slot(item), 0:1024]).then_inc(head.sem, head.step(item))
                    elif kind == "l1":
                        normalize(L, step[1], ("t", step[1]))
                    elif kind == "mkv":
                        act.wait_ge(m_done.sem, m_done.at(L, ("mkv", 1)))
                        for j in range(2):
                            copy(MKT[:, j, :], G[j][:, 0:MEM]).then_inc(copied.sem, copied.step(("mkv", j)))
                        for j in range(2):
                            copy(MV[:, j, :], G[2 + j][:, 0:BW]).then_inc(copied.sem, copied.step(("mkv", 2 + j)))
                    elif kind in ("xj", "mj"):
                        _, t, j = step
                        act.wait_ge(t_done.sem, t_done.at(L, step))
                        bank = TP if j == 0 else O
                        copy(XTH[:, 4 * j:4 * j + 4, t * P:(t + 1) * P], bank[:].rearrange("p (k n) -> p k n", k=4)).then_inc(moved.sem, moved.step(step))
                    elif kind == "yj":
                        _, b, t = step
                        act.wait_ge(t_done.sem, t_done.at(L, step))
                        copy(YTH[:, :, t * P:(t + 1) * P], TP[:, 0:2 * P].rearrange("p (k n) -> p k n", k=2)).then_inc(moved.sem, moved.step(step))
                    elif kind in ("ej", "ixj", "qk", "cj", "dj"):
                        t = step[-1]
                        q = slice(t * P, (t + 1) * P)
                        act.wait_ge(t_done.sem, t_done.at(L, step))
                        tp = TP[:].rearrange("p (k n) -> p k n", k=4)
                        if kind == "ej":
                            copy(QK2[:, 0:2, q], tp[:, 0:2, :]).then_inc(moved.sem, moved.step(step))
                        elif kind == "ixj":
                            copy(QK2[:, 2:4, q], tp[:, 0:2, :]).then_inc(moved.sem, moved.step(("ixq", t)))
                            copy(QK[:, 0, q], tp[:, 2, :]).then_inc(moved.sem, moved.step(step))
                        elif kind == "qk":
                            copy((QK2 if step[1] == "A" else QK)[:, :, q], tp).then_inc(moved.sem, moved.step(step))
                        elif kind == "cj":
                            copy(QK2[:, 0:3, q], tp[:, 0:3, :]).then_inc(moved.sem, moved.step(step))
                        else:
                            copy(QK[0:HD + MR, :, q], tp[0:HD + MR, :, :]).then_inc(moved.sem, moved.step(step))
                            act.wait_ge(t_done.sem, t_done.at(L, ("dk", t)))
                            copy(QK2[0:HD + MR, :, q], O[0:HD + MR, :].rearrange("p (k n) -> p k n", k=4)).then_inc(moved.sem, moved.step(("dk", t)))
                    elif kind == "du":
                        t = step[1]
                        act.wait_ge(m_done.sem, m_done.at(L, step))
                        copy(ST[:, t, 0:384], O[:, 0:384]).then_inc(copied.sem, copied.step(("dq", t)))
                        kv = TP[:].rearrange("p (h c) -> p h c", h=NH)
                        copy(VZ[:, 1, t, 0:BW].rearrange("p (h c) -> p h c", h=NH), kv[:, :, HD:2 * HD]).then_inc(copied.sem, copied.step(("dv", t)))
                        if t >= 2:
                            act.wait_ge(t_done.sem, t_done.at(L, ("dk", t - 2)))
                        copy(KC[:, t % 2, :, 0:HD], kv[:, :, 0:HD]).then_inc(copied.sem, copied.step(("dk", t)))
                    elif kind == "I":
                        _, t, h = step
                        w = (t + 1) * P
                        s = th_slot(L, step)
                        act.wait_ge(s_done.sem, s_done.at(L, step))
                        nc.scalar.activation(TH[:, s, 0:w], U[:, 0:w], ACT.Relu).then_inc(act_out.sem, act_out.step(step))
                    elif kind == "S":
                        _, b, u = step
                        t, j, w = unit(b, u)
                        act.wait_ge(masked.sem, masked.at(L, (b, u)))
                        nc.scalar.activation(SM[:, u % 2, 0:w], SM[:, u % 2, 0:w], ACT.Exp, bias=NMX[:, u % 2:u % 2 + 1],
                                             scale=SCALE[b], accum_out=RS[:, t % 2, j:j + 1]).then_inc(exped.sem, exped.step((b, u)))
                    elif kind == "T":
                        _, b, u = step
                        t, j, w = unit(b, u)
                        act.wait_ge(t_done.sem, t_done.at(L, step))
                        copy(PT[:, 0:w], TP[:, 0:w]).then_inc(moved.sem, moved.step(step))
                    elif kind == "R":
                        t = step[1]
                        act.wait_ge(summed.sem, summed.at(L, ("Cn", t)))
                        nc.scalar.activation(SS[:, 4:8], SS[:, 0:4], ACT.Sqrt, scale=1.0 / HD,
                                             bias=CN[:, C_RE:C_RE + 1]).then_inc(rooted.sem, rooted.step(("C", t)))
                    elif kind == "grp":
                        _, c, kh, t, part = step
                        if kh == 0 or part == 0:
                            continue
                        if c in ("A0", "B0", "C0"):
                            act.wait_ge(gemm.sem, gemm.at(L, (c, 1, t)))
                            copy(ST[:, t, :], G[t][:]).then_inc(copied.sem, copied.step((c, t)))
                        elif c == "IX":
                            act.wait_ge(gemm.sem, gemm.at(L, (c, 1, t)))
                            copy(IW[:, t, :], G[t][:, 288:296], scale=(IH * ID) ** -0.5).then_inc(copied.sem, copied.step(("iw", t)))
                            copy(ST[:, t, 0:288], G[t][:, 0:288]).then_inc(copied.sem, copied.step((c, t)))
                        elif c in ("E", "A1", "B1", "C1", "D1"):
                            s = th_slot(L, (c, t))
                            act.wait_ge(gemm.sem, gemm.at(L, (c, 1, t)))
                            z0 = 0 if c == "D1" else BW
                            nc.scalar.activation(TH[:, s, 0:BW], G[t][:, z0:z0 + BW], ACT.Tanh, scale=0.5).then_inc(act_out.sem, act_out.step((c, t)))
                            if c != "D1":
                                copy(VZ[:, vz(c[0]), t, 0:BW], G[t][:, 0:BW]).then_inc(copied.sem, copied.step((c, t)))
                        elif c == "D0":
                            if t == 0:
                                act.wait_ge(summed.sem, summed.at(L, ("lam",)))
                                nc.scalar.activation(LAM[:, 2:4], LAM[:, 0:2], ACT.Exp).then_inc(rooted.sem, rooted.step(("lam",)))
                            act.wait_ge(gemm.sem, gemm.at(L, (c, 1, t)))
                            copy(ST[:, t, 384:416], G[t][:, 384:416]).then_inc(copied.sem, copied.step((c, t)))
                            chain(nc.scalar.activation(JNK, G[t][:, 0:QL], ACT.Square, accum_out=MS[:, t, 0:1]))
                            chain(nc.scalar.activation(JNK[:, 0:KVL], G[t][:, QL:QL + KVL], ACT.Square, accum_out=MS[:, t, 1:2]))
                            nc.scalar.activation(MS[:, t, 2:3], MS[:, t, 0:1], ACT.Sqrt, scale=1.0 / QL,
                                                 bias=CN[:, C_RE:C_RE + 1]).then_inc(rooted.sem, rooted.step(("cq", t)))
                            nc.scalar.activation(MS[:, t, 3:4], MS[:, t, 1:2], ACT.Sqrt, scale=1.0 / KVL,
                                                 bias=CN[:, C_RE:C_RE + 1]).then_inc(rooted.sem, rooted.step(("D0", t)))
                        elif c[0] == "g":
                            s = th_slot(L, (c, t))
                            act.wait_ge(gemm.sem, gemm.at(L, (c, 1, t)))
                            nc.scalar.activation(TH[:, s, :], G[t][:], ACT.Tanh, scale=0.5).then_inc(act_out.sem, act_out.step((c, t)))
                        elif c == "O1":
                            act.wait_ge(summed.sem, summed.at(L, ("ln", t)))
                            nc.scalar.activation(SS[:, 12 + t:13 + t], BN[:, 4 * t + 1:4 * t + 2], ACT.Sqrt,
                                                 bias=CN[:, C_EPS + 1:C_EPS + 2]).then_inc(rooted.sem, rooted.step(("ln", t)))

        @block.vector
        def _(dve):
            th_n = [0]
            latest = []

            def note(tally, key):
                latest[:] = [tally, tally.n + 1]
                return tally.step(key)

            def settle():
                if latest:
                    dve.wait_ge(latest[0].sem, latest[1])

            def chain(ins):
                ins.then_inc(v_chain.sem, v_chain.step(("n",)))
                dve.wait_ge(v_chain.sem, v_chain.n)

            def rotate(xv, heads, half, t, off, ticks):
                cc, sn, sp_ = rope(t, off, half)
                r = DS[:, 0:heads * 2 * half].rearrange("p (h r) -> p h r", h=heads)
                chain(nc.vector.tensor_tensor(r[:, :, 0:half], xv[:, :, half:2 * half],
                                              sn.unsqueeze(1).to_broadcast([P, heads, half]), ALU.mult))
                chain(nc.vector.tensor_tensor(r[:, :, half:2 * half], xv[:, :, 0:half],
                                              sp_.unsqueeze(1).to_broadcast([P, heads, half]), ALU.mult))
                chain(nc.vector.tensor_tensor(xv[:, :, 0:2 * half], xv[:, :, 0:2 * half],
                                              cc.unsqueeze(1).to_broadcast([P, heads, 2 * half]), ALU.mult))
                ins = nc.vector.tensor_tensor(xv[:, :, 0:2 * half], xv[:, :, 0:2 * half], r, ALU.add)
                if ticks is None:
                    chain(ins)
                else:
                    ins.then_inc(roped.sem, note(roped, ticks))

            def stats(t, key):
                for j in range(2):
                    chain(nc.vector.bn_stats(DS[:, 6 * j:6 * j + 6], X[:, t, j * 512:(j + 1) * 512]))
                nc.vector.bn_aggr(BN[:, 4 * t:4 * t + 2], DS[:, 0:12]).then_inc(summed.sem, note(summed, key))

            def scale(L, t, root_key, key):
                dve.wait_ge(rooted.sem, rooted.at(L, root_key))
                chain(nc.vector.reciprocal(BN[:, 4 * t + 2:4 * t + 3], SS[:, 12 + t:13 + t]))
                nc.vector.scalar_tensor_tensor(out=BN[:, 4 * t + 3:4 * t + 4], in0=BN[:, 4 * t:4 * t + 1], scalar=-1.0,
                                               in1=BN[:, 4 * t + 2:4 * t + 3], op0=ALU.mult,
                                               op1=ALU.mult).then_inc(summed.sem, note(summed, key + ("scale",)))

            def gain(L, t, key, g):
                dve.wait_ge(scaled.sem, scaled.at(L, key))
                nc.vector.tensor_tensor(X[:, t, :], X[:, t, :], g, ALU.mult).then_inc(gained.sem, note(gained, key))

            dve.wait_ge(first_in.sem, first_in.at(0, ("first", "c")))
            for t in range(NT):
                dve.wait_ge(x_in[t].sem, x_in[t].at(0, ("first", t)))
                settle()
                stats(t, ("first", t))
                scale(0, t, ("first", t), ("first", t))
                if t > 0:
                    gain(0, t - 1, ("first", t - 1), LN_IN[:, 0:D])
                else:
                    dve.wait_ge(first_ln_in.sem, first_ln_in.at(0, ("first", 1)))
            gain(0, NT - 1, ("first", NT - 1), LN_IN[:, 0:D])
            for L in range(DEPTH):
                new_layer([masked, used, gated, roped, final, rest, summed, residual, gained, v_chain], L)
                for step in PLAN:
                    kind = step[0]
                    settle()
                    if kind == "rms":
                        t = step[1]
                        dve.wait_ge(rooted.sem, rooted.at(L, ("D0", t)))
                        chain(nc.vector.reciprocal(RI[:, 0:2], MS[:, t, 2:4]))
                        chain(nc.vector.scalar_tensor_tensor(out=ST[:, t, 0:QL], in0=G[t][:, 0:QL], scalar=RI[:, 0:1],
                                                     in1=PRM[:, 0:QL], op0=ALU.mult, op1=ALU.mult))
                        rotate(ST[:, t, 384:416].rearrange("p (h c) -> p h c", h=1), 1, MR // 2, t, RM, ("kr", t))
                        dve.wait_ge(roped.sem, roped.at(L, ("kr", t)))
                        nc.vector.scalar_tensor_tensor(out=ST[:, t, QL:QL + KVL], in0=G[t][:, QL:QL + KVL], scalar=RI[:, 1:2],
                                                   in1=PRM[:, QL:QL + KVL], op0=ALU.mult, op1=ALU.mult).then_inc(gated.sem, note(gated, ("D0", t)))
                    elif kind == "l1":
                        scale(L, step[1], ("ln", step[1]), ("t", step[1]))
                    elif kind == "l2":
                        gain(L, step[1], ("t", step[1]), LN_IN[:, 0:D])
                    elif kind in ("xj", "mj"):
                        _, t, j = step
                        dve.wait_ge(moved.sem, moved.at(L, step))
                        bank = TP if j == 0 else O
                        q = slice(t * P, (t + 1) * P)
                        nc.vector.tensor_tensor(XTL[:, 4 * j:4 * j + 4, q], bank[:].rearrange("p (k n) -> p k n", k=4),
                                                XTH[:, 4 * j:4 * j + 4, q].bitcast(F32), ALU.subtract).then_inc(rest.sem, note(rest, (kind[0], t, j)))
                    elif kind == "yj":
                        _, b, t = step
                        dve.wait_ge(moved.sem, moved.at(L, step))
                        q = slice(t * P, (t + 1) * P)
                        nc.vector.tensor_tensor(YTL[:, :, q], TP[:, 0:2 * P].rearrange("p (k n) -> p k n", k=2),
                                                YTH[:, :, q].bitcast(F32), ALU.subtract).then_inc(rest.sem, note(rest, ("y", b, t)))
                    elif kind == "du":
                        t = step[1]
                        dve.wait_ge(copied.sem, copied.at(L, ("dk", t)))
                        nc.vector.tensor_copy(KC[:, t % 2, :, HD:HD + MR],
                                              ST[:, t, 384:416].unsqueeze(1).to_broadcast([P, NH, MR])).then_inc(v_chain.sem, v_chain.step(("n",)))
                        rotate(ST[:, t, 0:384].rearrange("p (h c) -> p h c", h=NH)[:, :, HD:HD + MR], NH, MR // 2, t, RM, ("dq", t))
                    elif kind == "I":
                        _, t, h = step
                        w, s = (t + 1) * P, th_n[0] % 2
                        th_n[0] += 1
                        dst = SC[:, SC_W[t]:SC_W[t] + w]
                        dve.wait_ge(act_out.sem, act_out.at(L, step))
                        if h == 0:
                            nc.vector.tensor_scalar(dst, TH[:, s, 0:w], IW[:, t, h:h + 1], 0.0, ALU.mult, ALU.add).then_inc(used.sem, note(used, step))
                        else:
                            dve.wait_ge(used.sem, used.at(L, ("I", t, h - 1)))
                            nc.vector.scalar_tensor_tensor(out=dst, in0=TH[:, s, 0:w], scalar=IW[:, t, h:h + 1], in1=dst,
                                                           op0=ALU.mult, op1=ALU.add).then_inc(used.sem, note(used, step))
                        if h == IH - 1:
                            dve.wait_ge(used.sem, used.at(L, step))
                            chain(nc.vector.tensor_tensor(dst[:, t * P:w], dst[:, t * P:w], mask(P), ALU.add))
                    elif kind == "K":
                        _, t, r = step
                        dst = SC[:, SC_W[t]:SC_W[t] + (t + 1) * P]
                        chain(nc.vector.max(TOP[:], dst))
                        chain(nc.vector.match_replace(dst, TOP[:], dst, TAKEN))
                    elif kind == "KB":
                        chain(nc.vector.tensor_scalar(SC[:], SC[:], TAKEN / 2, MASKED, ALU.is_gt, ALU.mult))
                    elif kind == "S":
                        _, b, u = step
                        t, j, w = unit(b, u)
                        dve.wait_ge(s_done.sem, s_done.at(L, step))
                        if b == "A" and t > 0:
                            bias = SC[:, SC_W[t]:SC_W[t] + w]
                        elif b == "E":
                            bias = CN[:, C_MASK:C_MASK + w]
                        else:
                            bias = mask(w)
                        chain(nc.vector.tensor_tensor_reduce(SM[:, u % 2, 0:w], S[:, 0:w], bias, 1.0, TAKEN, ALU.add, ALU.max,
                                                             NMX[:, 2 + u % 2:3 + u % 2]))
                        nc.vector.tensor_scalar(NMX[:, u % 2:u % 2 + 1], NMX[:, 2 + u % 2:3 + u % 2], -SCALE[b], None,
                                                ALU.mult).then_inc(masked.sem, note(masked, (b, u)))
                    elif kind == "V":
                        _, b, u = step
                        t, j, w = unit(b, u)
                        z = VZ[:, vz(b), t, BW:2 * BW]
                        if b != "C" and j == 3:
                            dve.wait_ge(used.sem, used.at(L, (b + "1" if b != "E" else b, t)))
                            dve.wait_ge(v_done.sem, v_done.at(L, (b, u)))
                            chain(nc.vector.reciprocal(RI[:, 0:4], RS[:, t % 2, 0:4]))
                            chain(nc.vector.tensor_tensor(DS[:, 0:BW].rearrange("p (h c) -> p h c", h=NH),
                                                          O[:, 0:BW].rearrange("p (h c) -> p h c", h=NH),
                                                          RI[:, 0:4].unsqueeze(2).to_broadcast([P, NH, HD]), ALU.mult))
                            nc.vector.scalar_tensor_tensor(out=z, in0=DS[:, 0:BW], scalar=0.5, in1=z, op0=ALU.mult,
                                                           op1=ALU.mult).then_inc(final.sem, note(final, (b, t)))
                        if b == "C" and j == 7:
                            dve.wait_ge(v_done.sem, v_done.at(L, (b, u)))
                            chain(nc.vector.reciprocal(RI[:], RS[:, t % 2, :]))
                            odd = RI[:].rearrange("p (h c) -> p h c", c=2)[:, :, 1]
                            chain(nc.vector.tensor_scalar(odd, odd, LAM[:, 4:5], None, ALU.mult))
                            nc.vector.tensor_tensor(DS[:].rearrange("p (h c) -> p h c", h=8),
                                                    O[:].rearrange("p (h c) -> p h c", h=8),
                                                    RI[:].unsqueeze(2).to_broadcast([P, 8, HD]), ALU.mult).then_inc(summed.sem, note(summed, ("C", t)))
                            dve.wait_ge(summed.sem, summed.at(L, ("C", t)))
                            ds = DS[:].rearrange("p (h c d) -> p h c d", h=NH, c=2)
                            df = DF[:].rearrange("p (h c) -> p h c", h=NH)
                            chain(nc.vector.tensor_tensor(df, ds[:, :, 0, :], ds[:, :, 1, :], ALU.add))
                            chain(nc.vector.tensor_tensor(DS[:, 0:BW], DF[:], DF[:], ALU.mult))
                            nc.vector.tensor_reduce(SS[:, 0:4], DS[:, 0:BW].rearrange("p (h c) -> p h c", h=NH), AX.X,
                                                    ALU.add).then_inc(summed.sem, note(summed, ("Cn", t)))
                    elif kind == "F":
                        t = step[1]
                        z, df = VZ[:, 0, t, BW:2 * BW], DF[:].rearrange("p (h c) -> p h c", h=NH)
                        dve.wait_ge(rooted.sem, rooted.at(L, ("C", t)))
                        chain(nc.vector.reciprocal(RI[:, 0:4], SS[:, 4:8]))
                        chain(nc.vector.tensor_tensor(df, df, RI[:, 0:4].unsqueeze(2).to_broadcast([P, NH, HD]), ALU.mult))
                        chain(nc.vector.tensor_tensor(df, df, DN[:].unsqueeze(1).to_broadcast([P, NH, HD]), ALU.mult))
                        nc.vector.tensor_tensor(z, z, DF[:], ALU.mult).then_inc(final.sem, note(final, ("C", t)))
                    elif kind == "grp":
                        _, c, kh, t, part = step
                        if kh == 0 or part == 0:
                            continue
                        if c in ("A0", "B0"):
                            dve.wait_ge(copied.sem, copied.at(L, (c, t)))
                            rotate(ST[:, t, :].rearrange("p (h c) -> p h c", h=8), 8, 8, t, R64, (c, t))
                        elif c == "C0":
                            dve.wait_ge(copied.sem, copied.at(L, (c, t)))
                            rotate(ST[:, t, :].rearrange("p (h c) -> p h c", h=16), 16, 4, t, R32, (c, t))
                        elif c == "IX":
                            dve.wait_ge(copied.sem, copied.at(L, (c, t)))
                            rotate(ST[:, t, 0:288].rearrange("p (h c) -> p h c", h=9), 9, 4, t, R32, None)
                            nc.vector.tensor_copy(ST[:, t, 288:384].rearrange("p (r c) -> p r c", r=3),
                                                  ST[:, t, 256:288].unsqueeze(1).to_broadcast([P, 3, ID])).then_inc(roped.sem, note(roped, (c, t)))
                        elif c in ("E", "A1", "B1", "C1", "D1"):
                            s = th_n[0] % 2
                            th_n[0] += 1
                            z0 = 0 if c == "D1" else BW
                            dve.wait_ge(act_out.sem, act_out.at(L, (c, t)))
                            if c != "D1":
                                dve.wait_ge(copied.sem, copied.at(L, (c, t)))
                            nc.vector.scalar_tensor_tensor(out=VZ[:, vz(c[0]), t, BW:2 * BW], in0=TH[:, s, 0:BW], scalar=1.0,
                                                           in1=G[t][:, z0:z0 + BW], op0=ALU.add,
                                                           op1=ALU.mult).then_inc(used.sem, note(used, (c, t)))
                        elif c == "D0":
                            if t == 0:
                                dve.wait_ge(prm_copied.sem, prm_copied.at(L, ("prm",)))
                                dl = PRM[:, QL + KVL + HD:].rearrange("p (a b d) -> p a b d", a=2, b=2)
                                chain(nc.vector.tensor_tensor(DS[:, 0:2 * ID].rearrange("p (a d) -> p a d", a=2),
                                                              dl[:, :, 0, :], dl[:, :, 1, :], ALU.mult))
                                nc.vector.tensor_reduce(LAM[:, 0:2], DS[:, 0:2 * ID].rearrange("p (a d) -> p a d", a=2), AX.X,
                                                        ALU.add).then_inc(summed.sem, note(summed, ("lam",)))
                                dve.wait_ge(rooted.sem, rooted.at(L, ("lam",)))
                                chain(nc.vector.tensor_tensor(LAM[:, 5:6], LAM[:, 3:4], LAM[:, 2:3], ALU.subtract))
                                chain(nc.vector.tensor_tensor(LAM[:, 4:5], LAM[:, 5:6], CN[:, C_LAM + L:C_LAM + L + 1], ALU.add))
                                chain(nc.vector.tensor_scalar(DN[:], PRM[:, QL + KVL:QL + KVL + HD],
                                                              CN[:, C_LAM + DEPTH + L:C_LAM + DEPTH + L + 1], None, ALU.mult))
                        elif c[0] == "g":
                            s = th_n[0] % 2
                            th_n[0] += 1
                            cc = int(c[2])
                            m = M[:, t, cc * 512:(cc + 1) * 512]
                            dve.wait_ge(act_out.sem, act_out.at(L, (c, t)))
                            dve.wait_ge(u_done.sem, u_done.at(L, (c, t)))
                            if c[1] == "E":
                                nc.vector.scalar_tensor_tensor(out=m, in0=TH[:, s, :], scalar=1.0, in1=U[:], op0=ALU.add,
                                                               op1=ALU.mult).then_inc(used.sem, note(used, (c, t)))
                            else:
                                chain(nc.vector.scalar_tensor_tensor(out=TH[:, s, :], in0=TH[:, s, :], scalar=1.0, in1=U[:],
                                                                     op0=ALU.add, op1=ALU.mult))
                                nc.vector.tensor_tensor(m, m, TH[:, s, :], ALU.add).then_inc(used.sem, note(used, (c, t)))
                        elif c[0] == "O":
                            cc = int(c[1])
                            xc = X[:, t, cc * 512:(cc + 1) * 512]
                            dve.wait_ge(gemm.sem, gemm.at(L, (c, 1, t)))
                            nc.vector.scalar_tensor_tensor(out=xc, in0=G[t][:], scalar=0.5 / ALPHA, in1=xc, op0=ALU.mult,
                                                           op1=ALU.add).then_inc(residual.sem, note(residual, (c, t)))
                            if cc == 1:
                                dve.wait_ge(residual.sem, residual.at(L, (c, t)))
                                if t == 0:
                                    dve.wait_ge(ln_in.sem, ln_in.at(L, ("ln",)))
                                stats(t, ("ln", t))


_INS = ["x", "mem", "ln0_g", "ln0_b", "w_in", "mla_q_norm", "w_uq", "mla_kv_norm", "w_ukv", "diff_lam",
        "diff_norm", "w_mem_kv", "w_branch", "w_out", "ln_g", "ln_b"]


def kernel(**inputs):
    import numpy as _np
    import concourse.bacc as _bacc
    from concourse import mybir as _mybir
    from concourse.bass_utils import run_bass_kernel_spmd as _run

    arrays = {f"in_{name}_dram": _np.ascontiguousarray(inputs[name]) for name in _INS}
    arrays["shape_constants_dram"] = constants()
    known = {}
    for _ in range(2):
        nc = _bacc.Bacc("TRN2", target_bir_lowering=False, num_devices=1)
        args = [nc.dram_tensor(name, a.shape, _mybir.dt.from_np(a.dtype), kind="ExternalInput").ap()
                for name, a in arrays.items()]
        args.append(nc.dram_tensor("out_0_dram", (1, T, D), _mybir.dt.float32, kind="ExternalOutput").ap())
        build(nc, known, *args)
    r = _run(nc, [arrays], core_ids=[0])
    return r.results[0]["out_0_dram"]
```

```python
from contextlib import ExitStack

import numpy as np

import concourse.bass as bass
from concourse import mybir

F32 = mybir.dt.float32
F32R = mybir.dt.float32r
ALU = mybir.AluOpType
ACT = mybir.ActivationFunctionType
AX = mybir.AxisListType

P = 128
D = 1024
T = 512
DEPTH = 2
NT = T // P
KD = D // P
MEM = 256
NH = 4
HD = 64
BW = NH * HD
N_BRANCH = 5
IH, ID = 8, 32
TOPK = min(256, T // 4)
ROUNDS = TOPK // 8
QL, KVL = 256, 128
MR = 32
ROPE_THETA = 500000.0
ALPHA = (2 * DEPTH) ** 0.25
LN_EPS = 1e-5
RMS_EPS = 1e-6
MASKED = -1.0e30
TAKEN = -3.0e38

NAMES = [("a_q", BW), ("a_k", BW), ("a_v", BW), ("i_q", IH * ID), ("i_k", ID), ("i_w", IH),
         ("b_q", BW), ("b_k", BW), ("b_v", BW), ("c_q", BW), ("c_k", BW), ("c_v", BW),
         ("d_cq", QL), ("d_ckv", KVL), ("d_kr", MR), ("e_q", BW), ("z", N_BRANCH * BW), ("g", N_BRANCH * D)]
OFF = {}
_at = 0
for _n, _w in NAMES:
    OFF[_n] = _at
    _at += _w
IN_WIDTH = _at

BRANCH = {b: i for i, b in enumerate("ABCDE")}
SCALE = {"A": HD ** -0.5, "B": HD ** -0.5, "C": (HD // 2) ** -0.5, "D": (HD + MR) ** -0.5, "E": HD ** -0.5}
UNITS = NT * NH

CHUNKS = {
    "E": [(OFF["e_q"], BW), (OFF["z"] + 4 * BW, BW)],
    "IX": [(OFF["i_q"], IH * ID + ID + IH)],
    "A1": [(OFF["a_v"], BW), (OFF["z"], BW)], "A0": [(OFF["a_q"], 2 * BW)],
    "B1": [(OFF["b_v"], BW), (OFF["z"] + BW, BW)], "B0": [(OFF["b_q"], 2 * BW)],
    "C1": [(OFF["c_v"], BW), (OFF["z"] + 2 * BW, BW)], "C0": [(OFF["c_q"], 2 * BW)],
    "D0": [(OFF["d_cq"], QL + KVL + MR)], "D1": [(OFF["z"] + 3 * BW, BW)],
}
for _b in "ABCDE":
    for _c in range(2):
        CHUNKS[f"g{_b}{_c}"] = [(OFF["g"] + BRANCH[_b] * D + _c * 512, 512)]
WIDTH = {c: sum(w for _, w in r) for c, r in CHUNKS.items()}
WIDTH["O0"] = WIDTH["O1"] = 512
ORDER = ["IX", "E", "A1", "A0", "B1", "B0", "gE0", "gE1", "gB0", "gB1", "C0", "C1", "D0", "D1",
         "gA0", "gA1", "gC0", "gC1", "gD0", "gD1", "O0", "O1"]


LAG_T, LAG_V = 2, 3


def att_steps(b):
    out = []
    for i in range(UNITS + LAG_V):
        out.append([("V", b, i - LAG_V)] if i >= LAG_V else [])
        if 0 <= i - LAG_T < UNITS:
            out[-1].append(("T", b, i - LAG_T))
        out.append([("S", b, i)] if i < UNITS else [])
    return out


def diff_steps():
    out = []
    for i in range(UNITS + 5):
        first, second, third = [], [], []
        if i < UNITS:
            first.append(("S", "C", 2 * i))
            second.append(("S", "C", 2 * i + 1))
        if 0 <= i - 1 < UNITS:
            second.insert(0, ("W", i - 1))
            third.append(("T", "C", i - 1))
        if 0 <= i - 2 < UNITS:
            third.insert(0, ("V", "C", i - 2))
        out += [first, second, third]
    return [x for x in out if x]


PLACES = [
    ("top of tile 1", ("A1", 0, 0, 1), ("A0", 0, 2, 1), 0.0),
    ("index scores", ("E", 0, 2, 0), ("A0", 0, 2, 1), 0.0),
    ("index transposes", ("IX", 1, 3, 0), ("E", 0, 2, 1), 0.0),
    ("top of tile 2", ("A0", 1, 1, 0), ("B1", 1, 3, 1), 0.0),
    ("E queries", ("E", 1, 2, 1), ("A1", 0, 0, 1), 0.0),
    ("E attention", ("A1", 0, 0, 0), ("A0", 1, 2, 1), 0.0),
    ("A queries and keys", ("A0", 1, 3, 1), ("B1", 0, 1, 0), 0.0),
    ("top of tile 3", ("B0", 1, 0, 1), ("gE1", 1, 1, 1), 0.0),
    ("E out", ("B1", 0, 1, 1), ("B1", 1, 2, 1), 0.0),
    ("B out", ("gE1", 1, 1, 1), ("gB0", 0, 2, 0), 0.0),
    ("B queries and keys", ("B0", 1, 2, 1), ("gE0", 0, 1, 0), 0.0),
    ("B attention", ("gE0", 0, 0, 0), ("gE1", 1, 1, 0), -0.05),
    ("A out", ("gB1", 1, 3, 1), ("C0", 1, 1, 0), 0.0),
    ("A attention", ("gB0", 0, 1, 1), ("gB1", 1, 1, 1), 0.0),
    ("norm gains", ("gB0", 1, 3, 0), ("gB0", 1, 3, 0), 0.0),
    ("C queries and keys", ("C1", 0, 3, 0), ("C1", 1, 1, 1), 0.0),
    ("C attention", ("C1", 1, 0, 0), ("gA1", 0, 3, 1), 0.0),
    ("lambda", ("gB1", 1, 3, 1), ("C1", 0, 1, 0), 0.0),
    ("roots and C norms", ("gA1", 1, 0, 0), ("gA1", 1, 3, 0), 0.0),
    ("D heads", ("gA1", 1, 0, 0), ("gA1", 1, 3, 1), 0.0),
    ("D norms", ("D0", 1, 1, 0), ("D1", 0, 2, 1), 0.0),
    ("D latents", ("D1", 0, 2, 1), ("D1", 1, 2, 1), 0.0),
    ("C out", ("gC0", 0, 0, 0), ("gC0", 0, 3, 1), 0.0),
    ("D attention", ("gC0", 0, 2, 0), ("gD0", 0, 1, 1), -0.1),
    ("D out", ("gD0", 0, 0, 1), ("gD0", 1, 0, 0), 0.0),
]


def plan():
    groups = [(c, kh, t, part) for c in ORDER for kh in range(2) for t in range(NT) for part in range(2)]
    at = {g: i for i, g in enumerate(groups)}
    extra = [[] for _ in groups]

    def spread(steps, first, last, bend=0.0):
        a, b = at[first], at[last]
        for i, s in enumerate(steps):
            x = i / len(steps)
            extra[a + int((b - a + 1) * ((1 - bend) * x + bend * x * x) + 1e-6)].extend(s)

    halves = [(c, kh) for c in ORDER for kh in range(2)]
    for i in range(1, len(halves)):
        c, kh = halves[i - 1]
        extra[at[(c, kh, 0, 0)]].append(("split",) + halves[i] + (0,))
        extra[at[(c, kh, 1, 0)]].append(("split",) + halves[i] + (1,))
        if c[0] == "g" and kh == 0:
            extra[at[(c, 0, 1, 0)]].append(("splitb", c))
    start = [("split", ORDER[0], 0, 0), ("split", ORDER[0], 0, 1), ("mkv", 0), ("xj", 0, 0), ("xj", 0, 1), ("mkv", 1), ("xj", 1, 0), ("xj", 1, 1)]
    extra[at[(ORDER[0], 0, 0, 1)]] += [("xj", 2, 0), ("xj", 2, 1)]
    extra[at[(ORDER[0], 0, 1, 1)]] += [("xj", 3, 0), ("xj", 3, 1)]

    def tiles(*kind):
        return [[kind + (t,)] for t in range(NT)]

    idx = [[("I", t, h)] for t in range(1, NT) for h in range(IH)]
    tops = [[[(kind, t, r)] for r in range(ROUNDS) for kind in ("top", "take")] for t in range(NT)]
    steps_of = {
        "index transposes": tiles("ixj"), "index scores": idx, "top of tile 1": tops[1],
        "top of tile 2": tops[2], "top of tile 3": tops[3] + [[("KB",)]],
        "E queries": tiles("ej"), "E attention": att_steps("E"), "E out": tiles("yj", "E"),
        "A queries and keys": tiles("qk", "A"), "A attention": att_steps("A"), "A out": tiles("yj", "A"),
        "B queries and keys": tiles("qk", "B"), "B attention": att_steps("B"), "B out": tiles("yj", "B"),
        "C queries and keys": tiles("qk", "C"), "C attention": diff_steps(), "C out": tiles("yj", "C"),
        "D norms": tiles("rms"), "roots and C norms": [[("R",)]] + tiles("F"), "D latents": tiles("cj"),
        "D heads": [[("du", 0)], [("du", 1)], [("dj", 0)], [("du", 2)], [("dj", 1)], [("du", 3)], [("dj", 2)], [("dj", 3)]],
        "D attention": att_steps("D"), "D out": tiles("yj", "D"),
        "norm gains": [[("prm",)]], "lambda": [[("lam",)]],
    }
    for name, first, last, bend in PLACES:
        spread(steps_of[name], first, last, bend)
    extra[at[("gD1", 1, 2, 0)]] += [("mj", 0, 0), ("mj", 0, 1)]
    extra[at[("gD1", 1, 3, 0)]] += [("mj", 1, 0), ("mj", 1, 1)]
    extra[at[("O0", 0, 0, 1)]] += [("mj", 2, 0), ("mj", 2, 1)]
    extra[at[("O0", 0, 1, 1)]] += [("mj", 3, 0), ("mj", 3, 1)]
    extra[at[("O1", 1, 1, 1)]] += [("l1", 0)]
    extra[at[("O1", 1, 2, 1)]] += [("l1", 1), ("l2", 0)]
    extra[at[("O1", 1, 3, 1)]] += [("l1", 2), ("l2", 1), ("l1", 3), ("l2", 2), ("l2", 3)]
    steps = list(start)
    for g, more in zip(groups, extra):
        steps.append(("grp",) + g)
        steps += more
    return steps


PLAN = plan()
SPLITS = [(c, kh) for c in ORDER for kh in range(2)]


def loads():
    out = []
    for c in ORDER:
        if c == "gB1":
            out.append(("prm", 0))
        out.append((c, 0))
        out.append((c, 1))
        if c[0] == "g":
            out.append(("wb", c))
        if c == "gA1":
            out.append(("du", 0))
    return out


LOADS = loads()
NRAW, NW = 2, 2
assert len(LOADS) % NRAW == 0 and len(SPLITS) % NW == 0

C_ID, C_MASK = 0, P
C_ROPE = C_MASK + T
R64, R32, RM = 0, 32, 48
ROPE_W = 48 + 2 * MR
C_LAM = C_ROPE + NT * ROPE_W
C_EPS = C_LAM + 2 * DEPTH
C_RE = C_EPS + 2
C_N = C_RE + 1


def constants():
    c = np.zeros((P, C_N), np.float32)
    p = np.arange(P)
    c[:, C_MASK + T - P:C_MASK + T] = np.where(p[None, :] <= p[:, None], 0.0, MASKED)
    c[:, C_ID:C_ID + P] = np.eye(P)
    for t in range(NT):
        pos = (t * P + p).astype(np.float32)
        for off, rot in ((R64, 16), (R32, 8), (RM, MR)):
            inv = np.float32(ROPE_THETA) ** (-np.arange(0, rot, 2, dtype=np.float32) / np.float32(rot))
            ang = pos[:, None] * inv[None, :].astype(np.float32)
            co, si = np.cos(ang), np.sin(ang)
            at = C_ROPE + t * ROPE_W + off
            c[:, at:at + 2 * rot] = np.concatenate([co, co, -si, si], 1)
    for layer in range(DEPTH):
        init = 0.8 - 0.6 * float(np.exp(-0.3 * layer))
        c[:, C_LAM + layer] = -init
        c[:, C_LAM + DEPTH + layer] = (1.0 - init) * 0.5
    c[:, C_EPS] = LN_EPS
    c[:, C_EPS + 1] = LN_EPS / ALPHA ** 2
    c[:, C_RE] = RMS_EPS
    return c


class Tally:

    def __init__(self, sem, known):
        self.sem, self.n, self.base, self.known = sem, 0, 0, known

    def step(self, key, by=1):
        self.n += by
        self.known.setdefault(key, self.n - self.base if key[0] != "first" else self.n)
        return by

    def layer(self, layer):
        if layer == 1:
            self.known.setdefault("per_layer", self.n - self.base)
        if layer == 0:
            self.known["ahead"] = self.n
        self.base = self.n

    def at(self, layer, key):
        if key[0] == "first":
            return self.known.get(key, 1)
        return self.known.get("ahead", 0) + layer * self.known.get("per_layer", 0) + self.known.get(key, 1)


def build(nc, known, x, mem, ln0_g, ln0_b, w_in, mla_q_norm, w_uq, mla_kv_norm, w_ukv, diff_lam,
          diff_norm, w_mem_kv, w_branch, w_out, ln_g, ln_b, consts, out):
    with ExitStack() as ctx:
        def sb(name, shape, dt=F32):
            return ctx.enter_context(nc.sbuf_tensor(name, shape, dt))

        def tally(name):
            return Tally(ctx.enter_context(nc.semaphore(name)), known.setdefault(name, {}))

        X = sb("residual", [P, NT, D])
        XTH = sb("stationary_head", [P, KD, T], F32R)
        XTL = sb("stationary_rest", [P, KD, T], F32R)
        M = sb("merged", [P, NT, D])
        MK_RAW = M[:].rearrange("p t d -> p (t d)").rearrange("p (s k n) -> p s k n", s=2, k=4)
        RAW = sb("raw_weights", [P, NRAW, 4 * 512])
        WH = sb("weights_head", [P, NW, 4 * 512], F32R)
        WL = sb("weights_rest", [P, NW, 4 * 512], F32R)
        WBH = sb("branch_weights_head", [P, 2, 512], F32R)
        WBL = sb("branch_weights_rest", [P, 2, 512], F32R)
        ST = sb("staged_features", [P, NT, 512])
        VZ = sb("values_and_gates", [P, 2, NT, 512])
        KC = sb("mla_keys", [P, 2, NH, HD + MR])
        QK = sb("queries_keys_T", [P, 4, T])
        QK2 = sb("queries_keys_T2", [P, 4, T])
        YTH = sb("branch_out_T_head", [P, 2, T], F32R)
        YTL = sb("branch_out_T_rest", [P, 2, T], F32R)
        IX_STAGE = M[:, :, 0:(IH + 1) * 3 * ID].rearrange("p t (h r c) -> p t h r c", h=IH + 1, r=3)
        IX_Q = [None, YTH, YTL, WBH]
        IX_K = WBL[:, 0, :]
        SM = sb("probabilities", [P, 2, T])
        PT = sb("probabilities_T", [P, T])
        TH = sb("activated", [P, 2, 512])
        SC_W = [0, 0, 2 * P, 5 * P]
        SC = sb("index_scores", [P, 9 * P])
        IW = sb("index_weights", [P, NT, IH])
        LN_IN = VZ[:, 0, :, :].rearrange("p t n -> p (t n)")
        MEM_IN = VZ[:, 1, :, :].rearrange("p t n -> p (t n)").rearrange("p (t d) -> p t d", t=2)
        MEMT = sb("memory_T", [P, KD, MEM])
        MKT = sb("memory_keys_T", [P, 2, MEM])
        MV = sb("memory_values", [P, 2, BW])
        PRM_N = QL + KVL + HD + 4 * ID
        PRM = sb("layer_norms", [P, PRM_N])
        CN = sb("consts_sb", [P, C_N])
        JNK = KC[:].rearrange("p a h c -> p (a h c)")[:, 0:QL]
        DS = sb("vector_scratch", [P, 512])
        DF = sb("diff_out", [P, BW])
        MAPS = [SM[:, 0, :], SM[:, 1, :], SC[:, 0:T], SC[:, T:2 * T]]
        CF = sb("map_factors", [P, 4])
        NMX = sb("negated_maxima", [P, 4])
        RS = sb("row_sums", [P, 2, 8])
        RI = sb("reciprocals", [P, 8])
        DEV = sb("deviations", [P, NT])
        MS = sb("mla_norm_sums", [P, NT, 4])
        CS = sb("diff_norm_sums", [P, 2, NT, NH])
        BNS = sb("half_tile_stats", [P, NT, 12])
        BN = sb("norm_stats", [P, 16])
        LAM = sb("lambdas", [P, 8])
        DN = PRM[:, QL + KVL:QL + KVL + HD]
        TOP = sb("top_eight", [P, 8])

        G = [ctx.enter_context(nc.psum_tensor(f"product{i}", [P, 512], F32)) for i in range(NT)]
        U = ctx.enter_context(nc.psum_tensor("branch_product", [P, 512], F32))
        S = ctx.enter_context(nc.psum_tensor("scores", [P, 512], F32))
        TP = ctx.enter_context(nc.psum_tensor("transposed", [P, 512], F32))
        O = ctx.enter_context(nc.psum_tensor("context", [P, 512], F32))

        mk_in = [tally(f"memory_weights_loaded{i}") for i in range(2)]
        raw = [tally(f"raw_loaded{i}") for i in range(NRAW)]
        first_in = tally("consts_loaded")
        x_in = [tally(f"x_loaded{t}") for t in range(NT)]
        ident_in = tally("identity_loaded")
        mem_in = [tally(f"memory_loaded{t}") for t in range(2)]
        first_ln_in = tally("first_norm_loaded")
        ln_in = tally("layer_norm_loaded")
        stored = tally("stored")
        gemm = tally("product_done")
        u_done = tally("branch_product_done")
        s_done = tally("scores_done")
        t_done = tally("transposes_done")
        v_done = tally("context_done")
        m_done = tally("small_products_done")
        head = tally("head_split")
        act_out = tally("activated_ready")
        copied = tally("product_copied")
        exped = tally("probabilities_ready")
        moved = tally("transposed_moved")
        rooted = tally("root_ready")
        scaled = tally("residual_scaled")
        squared = tally("latents_squared")
        a_chain = tally("scalar_step")
        masked = tally("scores_masked")
        joined = tally("maps_joined")
        topped = tally("top_eight_taken")
        inverted = tally("roots_inverted")
        used = tally("activated_used")
        gated = tally("gates_ready")
        roped = tally("rotated")
        final = tally("branch_tile_ready")
        rest = tally("rest_of_stationary")
        summed = tally("squares_summed")
        residual = tally("residual_added")
        v_chain = tally("vector_step")
        gained = tally("gain_applied")
        lo_done = tally("rest_split")
        normed = tally("normed")
        prm_copied = tally("norms_copied")

        def new_layer(mine, layer):
            for c in mine:
                c.layer(layer)

        ident = CN[:, C_ID:C_ID + P]

        def mask(w):
            return CN[:, C_MASK + T - w:C_MASK + T]

        def rope(t, off, half):
            at = C_ROPE + t * ROPE_W + off
            return CN[:, at:at + 2 * half], CN[:, at + 2 * half:at + 3 * half], CN[:, at + 3 * half:at + 4 * half]

        def raw_slot(item):
            return LOADS.index(item) % NRAW

        def w_slot(c, kh):
            return SPLITS.index((c, kh)) % NW

        def half_view(buf, slot, c):
            w = WIDTH[c]
            return buf[:, slot, 0:4 * w].rearrange("p (k n) -> p k n", k=4)

        def unit(b, u, maps=1):
            t, j = divmod(u, NH * maps)
            return t, j, MEM if b == "E" else (t + 1) * P

        def score_unit(b, u):
            return unit(b, u, 2 if b == "C" else 1)

        def probs(b, u):
            return MAPS[u % 4] if b == "C" else MAPS[u % 2]

        def vz(b):
            return 0 if b in "AC" else 1

        def before(key_step):
            same = [s for s in PLAN if s[0] == key_step[0]]
            i = same.index(key_step)
            return same[i - 1] if i else None

        block = ctx.enter_context(nc.Block())

        @block.sync
        def _(sp):
            def load_x(t):
                sp.dma_start(X[:, t, :], x[0, t * P:(t + 1) * P, :]).then_inc(x_in[t].sem, x_in[t].step(("first", t), 16))

            def load_mk(L, kh):
                sp.dma_start(MK_RAW[:, kh], w_mem_kv[L, kh * 512:(kh + 1) * 512, :].rearrange(
                    "(k p) n -> p k n", p=P)).then_inc(mk_in[kh].sem, mk_in[kh].step(("mk",), 16))

            sp.dma_start(CN[:, 0:P], consts[:, 0:P]).then_inc(ident_in.sem, ident_in.step(("first", "i"), 16))
            for t in range(2):
                sp.dma_start(MEM_IN[:, t], mem[0, t * P:(t + 1) * P, :]).then_inc(mem_in[t].sem, mem_in[t].step(("first", "m"), 16))
            sp.dma_start(CN[:, P:], consts[:, P:]).then_inc(first_in.sem, first_in.step(("first", "c"), 16))
            load_x(0)
            new_layer(mk_in, 0)
            load_mk(0, 0)
            sp.dma_start(LN_IN[:, 0:D], ln0_g.partition_broadcast(P)).then_inc(first_ln_in.sem, first_ln_in.step(("first", 0), 16))
            load_x(1)
            sp.dma_start(LN_IN[:, D:2 * D], ln0_b.partition_broadcast(P)).then_inc(first_ln_in.sem, first_ln_in.step(("first", 1), 16))
            load_x(2)
            load_x(3)
            load_mk(0, 1)
            for L in range(DEPTH):
                new_layer([*raw, ln_in], L)
                for i, item in enumerate(LOADS):
                    s = i % NRAW
                    if i >= NRAW:
                        old, Lo = LOADS[i - NRAW], L
                    elif L > 0:
                        old, Lo = LOADS[len(LOADS) - NRAW + i], L - 1
                    else:
                        old, Lo = None, 0
                    if old is None:
                        pass
                    elif old[0] == "du":
                        sp.wait_ge(m_done.sem, m_done.at(Lo, ("du", NT - 1)))
                    elif old[0] == "prm":
                        sp.wait_ge(prm_copied.sem, prm_copied.at(Lo, ("prm",)))
                    else:
                        sp.wait_ge(lo_done.sem, lo_done.at(Lo, old))
                    if item == ("gD1", 0):
                        sp.wait_ge(t_done.sem, t_done.at(L, ("yj", "C", NT - 1)))
                        sp.dma_start(LN_IN[:, 0:D], ln_g[L].partition_broadcast(P)).then_inc(ln_in.sem, ln_in.step(("half",), 16))
                        sp.dma_start(LN_IN[:, D:2 * D], ln_b[L].partition_broadcast(P)).then_inc(ln_in.sem, ln_in.step(("ln",), 16))
                    sem = raw[s]
                    if item[0] == "wb":
                        b, c = BRANCH[item[1][1]], int(item[1][2])
                        sp.dma_start(RAW[:, s, 0:1024].rearrange("p (k n) -> p k n", k=2),
                                     w_branch[L, b, :, c * 512:(c + 1) * 512].rearrange("(k p) n -> p k n", p=P)).then_inc(sem.sem, sem.step(item, 16))
                    elif item[0] == "du":
                        sp.dma_start(RAW[:, s, 0:768].rearrange("p (k n) -> p k n", k=2),
                                     w_uq[L].rearrange("(k p) n -> p k n", p=P)).then_inc(sem.sem, sem.step(("half", "du"), 16))
                        sp.dma_start(RAW[:, s, 768:1280], w_ukv[L]).then_inc(sem.sem, sem.step(item, 16))
                    elif item[0] == "prm":
                        at = 0
                        for src, w in ((mla_q_norm[L], QL), (mla_kv_norm[L], KVL), (diff_norm[L], HD),
                                       (diff_lam[L].rearrange("a b -> (a b)"), 4 * ID)):
                            key = item if at + w == PRM_N else ("part", "prm", at)
                            sp.dma_start(RAW[:, s, at:at + w], src.partition_broadcast(P)).then_inc(sem.sem, sem.step(key, 16))
                            at += w
                    elif item[0][0] == "O":
                        c, kh = int(item[0][1]), item[1]
                        sp.dma_start(RAW[:, s, :].rearrange("p (k n) -> p k n", k=4),
                                     w_out[L, kh * 512:(kh + 1) * 512, c * 512:(c + 1) * 512].rearrange("(k p) n -> p k n", p=P)).then_inc(sem.sem, sem.step(item, 16))
                    else:
                        c, kh = item
                        view = half_view(RAW, s, c)
                        at, ranges = 0, CHUNKS[c]
                        for j, (c0, w) in enumerate(ranges):
                            key = item if j == len(ranges) - 1 else ("part", c, kh)
                            sp.dma_start(view[:, :, at:at + w],
                                         w_in[L, kh * 512:(kh + 1) * 512, c0:c0 + w].rearrange("(k p) n -> p k n", p=P)).then_inc(sem.sem, sem.step(key, 16))
                            at += w
                if L + 1 < DEPTH:
                    new_layer(mk_in, L + 1)
                    sp.wait_ge(t_done.sem, t_done.at(L, ("mj", NT - 1, 1)))
                    for kh in range(2):
                        load_mk(L + 1, kh)
            for t in range(NT):
                if t < NT - 1:
                    sp.wait_ge(normed.sem, normed.at(DEPTH - 1, ("t", t)))
                else:
                    sp.wait_ge(gained.sem, gained.at(DEPTH - 1, ("last",)))
                sp.dma_start(out[0, t * P:(t + 1) * P, :], X[:, t, :]).then_inc(stored.sem, stored.step(("first", t), 16))
            sp.wait_ge(stored.sem, stored.at(0, ("first", NT - 1)))

        @block.gpsimd
        def _(pool):
            def offset(L, t, key, b):
                pool.wait_ge(gained.sem, gained.at(L, key))
                nc.gpsimd.tensor_tensor(X[:, t, :], X[:, t, :], b, ALU.add).then_inc(normed.sem, normed.step(key))

            for t in range(NT - 1):
                offset(0, t, ("first", t), LN_IN[:, D:2 * D])
            for L in range(DEPTH):
                new_layer([lo_done, normed, prm_copied], L)
                for step in PLAN:
                    if step[0] == "l2" and step[1] < NT - 1:
                        offset(L, step[1], ("t", step[1]), LN_IN[:, D:2 * D])
                    if step[0] == "prm":
                        if L > 0:
                            pool.wait_ge(final.sem, final.at(L - 1, ("D", NT - 1)))
                        rw = raw[raw_slot(("prm", 0))]
                        pool.wait_ge(rw.sem, rw.at(L, ("prm", 0)))
                        nc.gpsimd.tensor_copy(PRM[:], RAW[:, raw_slot(("prm", 0)), 0:PRM_N]).then_inc(prm_copied.sem, prm_copied.step(("prm",)))
                    if step[0] == "split":
                        item, piece = step[1:3], step[3]
                        pool.wait_ge(head.sem, head.at(L, step))
                        sw, sr, n = w_slot(*item), raw_slot(item), 2 * WIDTH[item[0]]
                        half = slice(piece * n, (piece + 1) * n)
                        nc.gpsimd.tensor_tensor(WL[:, sw, half], RAW[:, sr, half], WH[:, sw, half].bitcast(F32),
                                                ALU.subtract).then_inc(lo_done.sem, lo_done.step(item if piece else step))
                    elif step[0] == "splitb":
                        item = ("wb", step[1])
                        pool.wait_ge(head.sem, head.at(L, item))
                        sr = raw_slot(item)
                        nc.gpsimd.tensor_tensor(WBL[:].rearrange("p k n -> p (k n)"), RAW[:, sr, 0:1024],
                                                WBH[:].rearrange("p k n -> p (k n)").bitcast(F32),
                                                ALU.subtract).then_inc(lo_done.sem, lo_done.step(item))

        @block.tensor
        def _(pe):
            freed = {}

            def claim(bank):
                if bank in freed:
                    c, L, key = freed.pop(bank)
                    pe.wait_ge(c.sem, c.at(L, key))

            def product3(dst, xh, xl, wh, wl, start, stop):
                nc.tensor.matmul(dst, xh, wh, start=start, stop=False)
                nc.tensor.matmul(dst, xh, wl, start=False, stop=False)
                return nc.tensor.matmul(dst, xl, wh, start=False, stop=stop)

            pe.wait_ge(ident_in.sem, ident_in.at(0, ("first", "i")))
            for t in range(2):
                pe.wait_ge(mem_in[t].sem, mem_in[t].at(0, ("first", "m")))
                for j in range(4):
                    for i in range(2):
                        last = nc.tensor.transpose(G[j][:, (2 * i + t) * P:(2 * i + t + 1) * P],
                                                   MEM_IN[:, t, (2 * j + i) * P:(2 * j + i + 1) * P], ident)
                    if t == 1:
                        last.then_inc(t_done.sem, t_done.step(("first", "mem", j)))
                        freed[f"G{j}"] = (moved, 0, ("first", j))
            for L in range(DEPTH):
                new_layer([gemm, u_done, s_done, t_done, v_done, m_done], L)
                for step in PLAN:
                    kind = step[0]
                    if kind == "grp":
                        _, c, kh, t, part = step
                        w = WIDTH[c]
                        if kh == 0 and part == 0:
                            claim(f"G{t}")
                        if c == ORDER[0] and kh == 0:
                            pe.wait_ge(rest.sem, rest.at(L, ("x", t, 1)))
                        if c[0] == "O" and kh == 0:
                            pe.wait_ge(rest.sem, rest.at(L, ("m", t, 1)))
                        if t == 0 and part == 0:
                            pe.wait_ge(lo_done.sem, lo_done.at(L, (c, kh)))
                        wh, wl = (half_view(b, w_slot(c, kh), c) for b in (WH, WL))
                        for k in range(2 * part, 2 * part + 2):
                            kk = 4 * kh + k
                            last = product3(G[t][:, 0:w], XTH[:, kk, t * P:(t + 1) * P], XTL[:, kk, t * P:(t + 1) * P],
                                            wh[:, k, :], wl[:, k, :], kk == 0, kk == KD - 1)
                        if part == 0:
                            continue
                        last.then_inc(gemm.sem, gemm.step((c, kh, t)))
                        if kh == 1:
                            if c in ("A0", "B0", "C0", "IX"):
                                freed[f"G{t}"] = (copied, L, (c, t))
                            elif c[0] == "g":
                                freed[f"G{t}"] = (act_out, L, (c, t))
                            elif c[0] == "O":
                                freed[f"G{t}"] = (residual, L, (c, t))
                            elif c == "D0":
                                freed[f"G{t}"] = (gated, L, (c, t))
                            else:
                                freed[f"G{t}"] = (used, L, (c, t))
                            if c[0] == "g":
                                claim("U")
                                if t == 0:
                                    pe.wait_ge(lo_done.sem, lo_done.at(L, ("wb", c)))
                                    pe.wait_ge(rest.sem, rest.at(L, ("y", c[1], NT - 1)))
                                for k in range(2):
                                    last = product3(U[:], YTH[:, k, t * P:(t + 1) * P], YTL[:, k, t * P:(t + 1) * P],
                                                    WBH[:, k, :], WBL[:, k, :], k == 0, k == 1)
                                last.then_inc(u_done.sem, u_done.step((c, t)))
                                freed["U"] = (used, L, (c, t))
                    elif kind == "mkv":
                        kh = step[1]
                        banks = [("G0", G[0]), ("G1", G[1]), ("U", U), ("S", S)]
                        if kh == 0:
                            for name, _ in banks:
                                claim(name)
                            if L == 0:
                                for j in range(4):
                                    pe.wait_ge(moved.sem, moved.at(0, ("first", j)))
                        pe.wait_ge(mk_in[kh].sem, mk_in[kh].at(L, ("mk",)))
                        for k in range(4):
                            kk = 4 * kh + k
                            for j in range(2):
                                nc.tensor.matmul(banks[j][1][:, 0:MEM], MK_RAW[:, kh, k, j * P:(j + 1) * P], MEMT[:, kk, :],
                                                 start=kk == 0, stop=kk == KD - 1)
                            for j in range(2):
                                last = nc.tensor.matmul(banks[2 + j][1][:, 0:BW], MEMT[:, kk, j * P:(j + 1) * P],
                                                        MK_RAW[:, kh, k, BW:2 * BW], start=kk == 0, stop=kk == KD - 1)
                        last.then_inc(m_done.sem, m_done.step(step))
                        for j, (name, _) in enumerate(banks):
                            freed[name] = (copied, L, ("mkv", j))
                    elif kind in ("xj", "mj"):
                        _, t, j = step
                        name, bank = ("TP", TP) if j == 0 else ("O", O)
                        claim(name)
                        if kind == "xj":
                            if L == 0 and t == NT - 1:
                                pe.wait_ge(gained.sem, gained.at(0, ("first", "last")))
                            elif L == 0:
                                pe.wait_ge(normed.sem, normed.at(0, ("first", t)))
                            elif t == NT - 1:
                                pe.wait_ge(gained.sem, gained.at(L - 1, ("last",)))
                            else:
                                pe.wait_ge(normed.sem, normed.at(L - 1, ("t", t)))
                            src = X
                        else:
                            pe.wait_ge(used.sem, used.at(L, ("gD1", t)))
                            src = M
                        for i in range(4):
                            k = 4 * j + i
                            last = nc.tensor.transpose(bank[:, i * P:(i + 1) * P], src[:, t, k * P:(k + 1) * P], ident)
                        last.then_inc(t_done.sem, t_done.step(step))
                        freed[name] = (rest, L, (kind[0], t, j))
                    elif kind == "yj":
                        _, b, t = step
                        claim("TP")
                        pe.wait_ge(final.sem, final.at(L, (b, t)))
                        for i in range(2):
                            last = nc.tensor.transpose(TP[:, i * P:(i + 1) * P], VZ[:, vz(b), t, BW + i * P:BW + (i + 1) * P], ident)
                        last.then_inc(t_done.sem, t_done.step(step))
                        freed["TP"] = (rest, L, ("y", b, t))
                    elif kind == "ixj":
                        t = step[1]
                        pe.wait_ge(roped.sem, roped.at(L, ("IX", t)))
                        for g, (name, bank) in enumerate((("TP", TP), ("S", S))):
                            if t == 0:
                                continue
                            claim(name)
                            for i in range(4):
                                last = nc.tensor.transpose(bank[0:3 * ID, i * P:(i + 1) * P],
                                                           IX_STAGE[:, t, 4 * g + i].rearrange("p r c -> p (r c)"), ident)
                            last.then_inc(t_done.sem, t_done.step(("ixq", t, g)))
                            freed[name] = (moved, L, ("ixq", t, g))
                        claim("U")
                        nc.tensor.transpose(U[0:3 * ID, 0:P], IX_STAGE[:, t, IH].rearrange("p r c -> p (r c)"),
                                            ident).then_inc(t_done.sem, t_done.step(step))
                        freed["U"] = (moved, L, step)
                    elif kind in ("ej", "qk", "cj", "dj"):
                        t = step[-1]
                        claim("TP")
                        if kind == "ej":
                            pe.wait_ge(copied.sem, copied.at(L, ("E", t)))
                            src, n, w = VZ[:, 1, t, :], 2, P
                        elif kind == "qk":
                            pe.wait_ge(roped.sem, roped.at(L, (step[1] + "0", t)))
                            src, n, w = ST[:, t, :], 4, P
                        elif kind == "cj":
                            pe.wait_ge(gated.sem, gated.at(L, ("D0", t)))
                            pe.wait_ge(roped.sem, roped.at(L, ("kr", t)))
                            src, n, w = ST[:, t, :], 3, P
                        else:
                            pe.wait_ge(roped.sem, roped.at(L, ("dq", t)))
                            src, n, w = ST[:, t, :], NH, HD + MR
                        for i in range(n):
                            last = nc.tensor.transpose(TP[0:w, i * P:(i + 1) * P], src[:, i * w:(i + 1) * w], ident)
                        last.then_inc(t_done.sem, t_done.step(step))
                        freed["TP"] = (moved, L, step)
                        if kind == "dj":
                            claim("S")
                            for i in range(n):
                                last = nc.tensor.transpose(S[0:w, i * P:(i + 1) * P], KC[:, t % 2, i, :], ident)
                            last.then_inc(t_done.sem, t_done.step(("dk", t)))
                            freed["S"] = (moved, L, ("dk", t))
                    elif kind == "du":
                        t = step[1]
                        claim("S")
                        claim("O")
                        if t == 0:
                            rw = raw[raw_slot(("du", 0))]
                            pe.wait_ge(rw.sem, rw.at(L, ("du", 0)))
                        pe.wait_ge(moved.sem, moved.at(L, ("cj", t)))
                        wv = RAW[:, raw_slot(("du", 0)), :]
                        for k in range(2):
                            nc.tensor.matmul(S[:, 0:384], QK2[:, k, t * P:(t + 1) * P], wv[:, k * 384:(k + 1) * 384],
                                             start=k == 0, stop=k == 1)
                        nc.tensor.matmul(O[:], QK2[:, 2, t * P:(t + 1) * P], wv[:, 768:1280],
                                         start=True, stop=True).then_inc(m_done.sem, m_done.step(step))
                        freed["S"] = (copied, L, ("dq", t))
                        freed["O"] = (copied, L, ("dk", t))
                    elif kind == "I":
                        _, t, h = step
                        claim("U")
                        if h == 0:
                            pe.wait_ge(moved.sem, moved.at(L, ("ixj", t)))
                        w = (t + 1) * P
                        nc.tensor.matmul(U[:, 0:w], IX_Q[t][0:3 * ID, h // 4, (h % 4) * P:(h % 4 + 1) * P], IX_K[0:3 * ID, 0:w],
                                         start=True, stop=True).then_inc(s_done.sem, s_done.step(step))
                        freed["U"] = (act_out, L, step)
                    elif kind == "S":
                        _, b, u = step
                        t, j, w = score_unit(b, u)
                        claim("S")
                        if j == 0:
                            need = {"E": ("ej", t), "D": ("dk", t)}.get(b, ("qk", b, t))
                            pe.wait_ge(moved.sem, moved.at(L, need))
                            if b == "E" and u == 0:
                                pe.wait_ge(copied.sem, copied.at(L, ("mkv", 3)))
                        q = slice(t * P, (t + 1) * P)
                        if b == "E":
                            r = slice(64 * (j % 2), 64 * (j % 2) + 64)
                            lhs, rhs, row = QK2[r, j // 2, q], MKT[r, j // 2, :], r.start
                        elif b == "D":
                            lhs, rhs, row = QK[0:HD + MR, j, q], QK2[0:HD + MR, j, 0:w], 0
                        elif b == "C":
                            r = slice(32 * (j % 4), 32 * (j % 4) + 32)
                            lhs, rhs, row = QK[r, j // 4, q], QK[r, 2 + j // 4, 0:w], r.start
                        else:
                            r = slice(64 * (j % 2), 64 * (j % 2) + 64)
                            qk = QK2 if b == "A" else QK
                            lhs, rhs, row = qk[r, j // 2, q], qk[r, 2 + j // 2, 0:w], r.start
                        nc.tensor.matmul(S[:, 0:w], lhs, rhs, start=True, stop=True,
                                         tile_position=(row, 0)).then_inc(s_done.sem, s_done.step(step))
                        freed["S"] = (masked, L, (b, u))
                    elif kind == "T":
                        _, b, u = step
                        t, j, w = unit(b, u)
                        claim("TP")
                        if b == "C":
                            pe.wait_ge(joined.sem, joined.at(L, ("W", u)))
                        else:
                            pe.wait_ge(exped.sem, exped.at(L, (b, u)))
                        src = probs(b, 2 * u if b == "C" else u)
                        for i in range(w // P):
                            last = nc.tensor.transpose(TP[:, i * P:(i + 1) * P], src[:, i * P:(i + 1) * P], ident)
                        last.then_inc(t_done.sem, t_done.step(step))
                        freed["TP"] = (moved, L, step)
                    elif kind == "V":
                        _, b, u = step
                        t, j, w = unit(b, u)
                        if j == 0:
                            claim("O")
                            if b == "D":
                                pe.wait_ge(copied.sem, copied.at(L, ("dk", t)))
                            elif b != "E":
                                pe.wait_ge(copied.sem, copied.at(L, (b + "1", t)))
                        pe.wait_ge(moved.sem, moved.at(L, ("T", b, u)))
                        for i in range(w // P):
                            v = MV[:, i, j * HD:(j + 1) * HD] if b == "E" else VZ[:, vz(b), i, j * HD:(j + 1) * HD]
                            last = nc.tensor.matmul(O[:, j * HD:(j + 1) * HD], PT[:, i * P:(i + 1) * P], v,
                                                    start=i == 0, stop=i == w // P - 1)
                        last.then_inc(v_done.sem, v_done.step((b, u)))
                        if j == NH - 1:
                            freed["O"] = (summed if b == "C" else final, L, (b, t))

        @block.scalar
        def _(act):
            th_n = [0]
            th_users = []

            def th_slot(L, key):
                n = th_n[0]
                if n >= 2:
                    Lo, ko = th_users[n - 2]
                    act.wait_ge(used.sem, used.at(Lo, ko))
                th_n[0] += 1
                th_users.append((L, key))
                return n % 2

            def copy(dst, src, scale=1.0):
                return nc.scalar.activation(dst, src, ACT.Copy, scale=scale)

            def chain(ins):
                ins.then_inc(a_chain.sem, a_chain.step(("n",)))
                act.wait_ge(a_chain.sem, a_chain.n)

            def normalize(L, t, key):
                act.wait_ge(summed.sem, summed.at(L, key + ("scale",)))
                nc.scalar.activation(X[:, t, :], X[:, t, :], ACT.Identity, bias=BN[:, 4 * t + 3:4 * t + 4],
                                     scale=BN[:, 4 * t + 2:4 * t + 3]).then_inc(scaled.sem, scaled.step(key))

            act.wait_ge(first_in.sem, first_in.at(0, ("first", "c")))
            for j in range(4):
                act.wait_ge(t_done.sem, t_done.at(0, ("first", "mem", j)))
                copy(MEMT[:, 2 * j:2 * j + 2, :], G[j][:].rearrange("p (k n) -> p k n", k=2)).then_inc(moved.sem, moved.step(("first", j)))
            for t in range(NT):
                act.wait_ge(summed.sem, summed.at(0, ("first", t)))
                nc.scalar.activation(DEV[:, t:t + 1], BN[:, 4 * t + 1:4 * t + 2], ACT.Sqrt,
                                     bias=CN[:, C_EPS:C_EPS + 1]).then_inc(rooted.sem, rooted.step(("first", t)))
                normalize(0, t, ("first", t))
            for L in range(DEPTH):
                new_layer([head, act_out, copied, exped, moved, rooted, scaled, squared, a_chain], L)
                for step in PLAN:
                    kind = step[0]
                    if kind == "split":
                        item, piece = step[1:3], step[3]
                        rw = raw[raw_slot(item)]
                        act.wait_ge(rw.sem, rw.at(L, item))
                        i = SPLITS.index(item)
                        if i >= NW:
                            act.wait_ge(gemm.sem, gemm.at(L, SPLITS[i - NW] + (NT - 1,)))
                        elif L > 0:
                            act.wait_ge(gemm.sem, gemm.at(L - 1, SPLITS[len(SPLITS) - NW + i] + (NT - 1,)))
                        n = 2 * WIDTH[item[0]]
                        half = slice(piece * n, (piece + 1) * n)
                        copy(WH[:, i % NW, half], RAW[:, raw_slot(item), half]).then_inc(head.sem, head.step(step))
                    elif kind == "splitb":
                        item = ("wb", step[1])
                        rw = raw[raw_slot(item)]
                        act.wait_ge(rw.sem, rw.at(L, item))
                        prev = before(step)
                        if prev:
                            act.wait_ge(u_done.sem, u_done.at(L, (prev[1], NT - 1)))
                        elif L > 0:
                            act.wait_ge(u_done.sem, u_done.at(L - 1, ("gD1", NT - 1)))
                        copy(WBH[:].rearrange("p k n -> p (k n)"), RAW[:, raw_slot(item), 0:1024]).then_inc(head.sem, head.step(item))
                    elif kind == "l1":
                        normalize(L, step[1], ("t", step[1]))
                    elif step == ("mkv", 1):
                        act.wait_ge(m_done.sem, m_done.at(L, ("mkv", 1)))
                        for j in range(2):
                            copy(MKT[:, j, :], G[j][:, 0:MEM]).then_inc(copied.sem, copied.step(("mkv", j)))
                        for j in range(2):
                            copy(MV[:, j, :], (U, S)[j][:, 0:BW]).then_inc(copied.sem, copied.step(("mkv", 2 + j)))
                    elif kind in ("xj", "mj"):
                        _, t, j = step
                        act.wait_ge(t_done.sem, t_done.at(L, step))
                        bank = TP if j == 0 else O
                        copy(XTH[:, 4 * j:4 * j + 4, t * P:(t + 1) * P], bank[:].rearrange("p (k n) -> p k n", k=4)).then_inc(moved.sem, moved.step(step))
                    elif kind == "yj":
                        _, b, t = step
                        act.wait_ge(t_done.sem, t_done.at(L, step))
                        copy(YTH[:, :, t * P:(t + 1) * P], TP[:, 0:2 * P].rearrange("p (k n) -> p k n", k=2)).then_inc(moved.sem, moved.step(step))
                    elif kind == "ixj":
                        t = step[1]
                        for g, bank in enumerate((TP, S)):
                            if t > 0:
                                act.wait_ge(t_done.sem, t_done.at(L, ("ixq", t, g)))
                                copy(IX_Q[t][0:3 * ID, g, :], bank[0:3 * ID, :]).then_inc(moved.sem, moved.step(("ixq", t, g)))
                        act.wait_ge(t_done.sem, t_done.at(L, step))
                        copy(IX_K[0:3 * ID, t * P:(t + 1) * P], U[0:3 * ID, 0:P]).then_inc(moved.sem, moved.step(step))
                    elif kind in ("ej", "qk", "cj", "dj"):
                        t = step[-1]
                        q = slice(t * P, (t + 1) * P)
                        act.wait_ge(t_done.sem, t_done.at(L, step))
                        tp = TP[:].rearrange("p (k n) -> p k n", k=4)
                        if kind == "ej":
                            copy(QK2[:, 0:2, q], tp[:, 0:2, :]).then_inc(moved.sem, moved.step(step))
                        elif kind == "qk":
                            copy((QK2 if step[1] == "A" else QK)[:, :, q], tp).then_inc(moved.sem, moved.step(step))
                        elif kind == "cj":
                            copy(QK2[:, 0:3, q], tp[:, 0:3, :]).then_inc(moved.sem, moved.step(step))
                        else:
                            copy(QK[0:HD + MR, :, q], tp[0:HD + MR, :, :]).then_inc(moved.sem, moved.step(step))
                            act.wait_ge(t_done.sem, t_done.at(L, ("dk", t)))
                            copy(QK2[0:HD + MR, :, q], S[0:HD + MR, :].rearrange("p (k n) -> p k n", k=4)).then_inc(moved.sem, moved.step(("dk", t)))
                    elif kind == "du":
                        t = step[1]
                        act.wait_ge(m_done.sem, m_done.at(L, step))
                        act.wait_ge(inverted.sem, inverted.at(L, ("D0",)))
                        copy(ST[:, t, 0:384], S[:, 0:384], MS[:, t, 2:3]).then_inc(copied.sem, copied.step(("dq", t)))
                        kv = O[:].rearrange("p (h c) -> p h c", h=NH)
                        copy(VZ[:, 1, t, 0:BW].rearrange("p (h c) -> p h c", h=NH), kv[:, :, HD:2 * HD], MS[:, t, 3:4]).then_inc(copied.sem, copied.step(("dv", t)))
                        if t >= 2:
                            act.wait_ge(t_done.sem, t_done.at(L, ("dk", t - 2)))
                        copy(KC[:, t % 2, :, 0:HD], kv[:, :, 0:HD], MS[:, t, 3:4]).then_inc(copied.sem, copied.step(("dk", t)))
                    elif kind == "I":
                        _, t, h = step
                        w = (t + 1) * P
                        s = th_slot(L, step)
                        act.wait_ge(s_done.sem, s_done.at(L, step))
                        nc.scalar.activation(TH[:, s, 0:w], U[:, 0:w], ACT.Relu).then_inc(act_out.sem, act_out.step(step))
                    elif kind == "S":
                        _, b, u = step
                        t, j, w = score_unit(b, u)
                        p, m = probs(b, u)[:, 0:w], u % 4
                        act.wait_ge(masked.sem, masked.at(L, (b, u)))
                        nc.scalar.activation(p, p, ACT.Exp, bias=NMX[:, m:m + 1],
                                             scale=-1.0, accum_out=RS[:, t % 2, j:j + 1]).then_inc(exped.sem, exped.step((b, u)))
                    elif kind == "T":
                        _, b, u = step
                        t, j, w = unit(b, u)
                        act.wait_ge(t_done.sem, t_done.at(L, step))
                        copy(PT[:, 0:w], TP[:, 0:w]).then_inc(moved.sem, moved.step(step))
                    elif kind == "lam":
                        act.wait_ge(summed.sem, summed.at(L, ("lam",)))
                        nc.scalar.activation(LAM[:, 2:4], LAM[:, 0:2], ACT.Exp).then_inc(rooted.sem, rooted.step(("lam",)))
                    elif kind == "R":
                        act.wait_ge(squared.sem, squared.at(L, ("D0", NT - 1)))
                        nc.scalar.activation(MS[:, :, 2:4], MS[:, :, 0:2], ACT.Sqrt,
                                             bias=CN[:, C_RE:C_RE + 1]).then_inc(rooted.sem, rooted.step(("D0",)))
                        act.wait_ge(summed.sem, summed.at(L, ("Cn", NT - 1)))
                        nc.scalar.activation(CS[:, 1], CS[:, 0], ACT.Sqrt, scale=1.0 / HD,
                                             bias=CN[:, C_RE:C_RE + 1]).then_inc(rooted.sem, rooted.step(("C",)))
                    elif kind == "grp":
                        _, c, kh, t, part = step
                        if kh == 0 or part == 0:
                            continue
                        if c in ("A0", "B0", "C0"):
                            act.wait_ge(gemm.sem, gemm.at(L, (c, 1, t)))
                            copy(ST[:, t, :], G[t][:]).then_inc(copied.sem, copied.step((c, t)))
                        elif c == "IX":
                            act.wait_ge(gemm.sem, gemm.at(L, (c, 1, t)))
                            copy(IW[:, t, :], G[t][:, 288:296], scale=(IH * ID) ** -0.5).then_inc(copied.sem, copied.step(("iw", t)))
                            copy(ST[:, t, 0:288], G[t][:, 0:288]).then_inc(copied.sem, copied.step((c, t)))
                        elif c in ("E", "A1", "B1", "C1", "D1"):
                            s = th_slot(L, (c, t))
                            act.wait_ge(gemm.sem, gemm.at(L, (c, 1, t)))
                            z0 = 0 if c == "D1" else BW
                            nc.scalar.activation(TH[:, s, 0:BW], G[t][:, z0:z0 + BW], ACT.Tanh, scale=0.5).then_inc(act_out.sem, act_out.step((c, t)))
                            if c != "D1":
                                copy(VZ[:, vz(c[0]), t, 0:BW], G[t][:, 0:BW]).then_inc(copied.sem, copied.step((c, t)))
                        elif c == "D0":
                            act.wait_ge(gemm.sem, gemm.at(L, (c, 1, t)))
                            copy(ST[:, t, 384:416], G[t][:, 384:416]).then_inc(copied.sem, copied.step((c, t)))
                            if t > 0:
                                act.wait_ge(squared.sem, squared.at(L, (c, t - 1)))
                            chain(nc.scalar.activation(JNK, G[t][:, 0:QL], ACT.Square, scale=QL ** -0.5, accum_out=MS[:, t, 0:1]))
                            nc.scalar.activation(JNK[:, 0:KVL], G[t][:, QL:QL + KVL], ACT.Square, scale=KVL ** -0.5,
                                                 accum_out=MS[:, t, 1:2]).then_inc(squared.sem, squared.step((c, t)))
                        elif c[0] == "g":
                            s = th_slot(L, (c, t))
                            act.wait_ge(gemm.sem, gemm.at(L, (c, 1, t)))
                            nc.scalar.activation(TH[:, s, :], G[t][:], ACT.Tanh, scale=0.5).then_inc(act_out.sem, act_out.step((c, t)))
                        elif c == "O1":
                            act.wait_ge(summed.sem, summed.at(L, ("ln", t)))
                            nc.scalar.activation(DEV[:, t:t + 1], BN[:, 4 * t + 1:4 * t + 2], ACT.Sqrt,
                                                 bias=CN[:, C_EPS + 1:C_EPS + 2]).then_inc(rooted.sem, rooted.step(("ln", t)))

        @block.vector
        def _(dve):
            th_n = [0]
            latest = []

            def note(tally, key):
                latest[:] = [tally, tally.n + 1]
                return tally.step(key)

            def settle():
                if latest:
                    dve.wait_ge(latest[0].sem, latest[1])

            def go(ins):
                ins.then_inc(v_chain.sem, v_chain.step(("n",)))

            def chain(ins):
                ins.then_inc(v_chain.sem, v_chain.step(("n",)))
                dve.wait_ge(v_chain.sem, v_chain.n)

            def rotate(xv, heads, half, t, off, ticks):
                cc, sn, sp_ = rope(t, off, half)
                n = heads * 2 * half
                r, c = (DS[:, i * n:(i + 1) * n].rearrange("p (h r) -> p h r", h=heads) for i in range(2))
                settle()
                go(nc.vector.tensor_tensor(r[:, :, 0:half], xv[:, :, half:2 * half],
                                           sn.unsqueeze(1).to_broadcast([P, heads, half]), ALU.mult))
                go(nc.vector.tensor_tensor(r[:, :, half:2 * half], xv[:, :, 0:half],
                                           sp_.unsqueeze(1).to_broadcast([P, heads, half]), ALU.mult))
                chain(nc.vector.tensor_tensor(c, xv[:, :, 0:2 * half],
                                              cc.unsqueeze(1).to_broadcast([P, heads, 2 * half]), ALU.mult))
                ins = nc.vector.tensor_tensor(xv[:, :, 0:2 * half], c, r, ALU.add)
                if ticks is None:
                    chain(ins)
                else:
                    ins.then_inc(roped.sem, note(roped, ticks))

            def half_stats(t, j):
                return nc.vector.bn_stats(BNS[:, t, 6 * j:6 * j + 6], X[:, t, j * 512:(j + 1) * 512])

            def stats(t, key):
                chain(half_stats(t, 1))
                nc.vector.bn_aggr(BN[:, 4 * t:4 * t + 2], BNS[:, t, :]).then_inc(summed.sem, note(summed, key))

            def scale(L, t, root_key, key):
                dve.wait_ge(rooted.sem, rooted.at(L, root_key))
                chain(nc.vector.reciprocal(BN[:, 4 * t + 2:4 * t + 3], DEV[:, t:t + 1]))
                nc.vector.scalar_tensor_tensor(out=BN[:, 4 * t + 3:4 * t + 4], in0=BN[:, 4 * t:4 * t + 1], scalar=-1.0,
                                               in1=BN[:, 4 * t + 2:4 * t + 3], op0=ALU.mult,
                                               op1=ALU.mult).then_inc(summed.sem, note(summed, key + ("scale",)))

            def gain(L, t, key, g):
                dve.wait_ge(scaled.sem, scaled.at(L, key))
                nc.vector.tensor_tensor(X[:, t, :], X[:, t, :], g, ALU.mult).then_inc(gained.sem, note(gained, key))

            dve.wait_ge(first_in.sem, first_in.at(0, ("first", "c")))
            for t in range(NT):
                dve.wait_ge(x_in[t].sem, x_in[t].at(0, ("first", t)))
                go(half_stats(t, 0))
                stats(t, ("first", t))
                if t == 1:
                    dve.wait_ge(first_ln_in.sem, first_ln_in.at(0, ("first", 1)))
                if t > 0:
                    gain(0, t - 1, ("first", t - 1), LN_IN[:, 0:D])
                scale(0, t, ("first", t), ("first", t))
            gain(0, NT - 1, ("first", NT - 1), LN_IN[:, 0:D])
            dve.wait_ge(gained.sem, gained.at(0, ("first", NT - 1)))
            nc.vector.tensor_tensor(X[:, NT - 1, :], X[:, NT - 1, :], LN_IN[:, D:2 * D],
                                    ALU.add).then_inc(gained.sem, note(gained, ("first", "last")))
            for L in range(DEPTH):
                new_layer([masked, joined, topped, inverted, used, gated, roped, final, rest, summed, residual, gained, v_chain], L)
                for step in PLAN:
                    kind = step[0]
                    if kind == "rms":
                        t = step[1]
                        dve.wait_ge(squared.sem, squared.at(L, ("D0", t)))
                        nc.vector.tensor_tensor(ST[:, t, 0:QL + KVL], G[t][:, 0:QL + KVL], PRM[:, 0:QL + KVL],
                                                ALU.mult).then_inc(gated.sem, note(gated, ("D0", t)))
                        rotate(ST[:, t, 384:416].rearrange("p (h c) -> p h c", h=1), 1, MR // 2, t, RM, ("kr", t))
                    elif kind == "l1":
                        scale(L, step[1], ("ln", step[1]), ("t", step[1]))
                    elif kind == "l2":
                        gain(L, step[1], ("t", step[1]), LN_IN[:, 0:D])
                        if step[1] == NT - 1:
                            dve.wait_ge(gained.sem, gained.at(L, ("t", NT - 1)))
                            nc.vector.tensor_tensor(X[:, NT - 1, :], X[:, NT - 1, :], LN_IN[:, D:2 * D],
                                                    ALU.add).then_inc(gained.sem, note(gained, ("last",)))
                    elif kind in ("xj", "mj"):
                        _, t, j = step
                        dve.wait_ge(moved.sem, moved.at(L, step))
                        bank = TP if j == 0 else O
                        q = slice(t * P, (t + 1) * P)
                        nc.vector.tensor_tensor(XTL[:, 4 * j:4 * j + 4, q], bank[:].rearrange("p (k n) -> p k n", k=4),
                                                XTH[:, 4 * j:4 * j + 4, q].bitcast(F32), ALU.subtract).then_inc(rest.sem, note(rest, (kind[0], t, j)))
                    elif kind == "yj":
                        _, b, t = step
                        dve.wait_ge(moved.sem, moved.at(L, step))
                        q = slice(t * P, (t + 1) * P)
                        nc.vector.tensor_tensor(YTL[:, :, q], TP[:, 0:2 * P].rearrange("p (k n) -> p k n", k=2),
                                                YTH[:, :, q].bitcast(F32), ALU.subtract).then_inc(rest.sem, note(rest, ("y", b, t)))
                    elif kind == "du":
                        t = step[1]
                        dve.wait_ge(copied.sem, copied.at(L, ("dk", t)))
                        nc.vector.tensor_copy(KC[:, t % 2, :, HD:HD + MR],
                                              ST[:, t, 384:416].unsqueeze(1).to_broadcast([P, NH, MR])).then_inc(v_chain.sem, v_chain.step(("n",)))
                        rotate(ST[:, t, 0:384].rearrange("p (h c) -> p h c", h=NH)[:, :, HD:HD + MR], NH, MR // 2, t, RM, ("dq", t))
                    elif kind == "I":
                        _, t, h = step
                        w, s = (t + 1) * P, th_n[0] % 2
                        th_n[0] += 1
                        dst = SC[:, SC_W[t]:SC_W[t] + w]
                        dve.wait_ge(act_out.sem, act_out.at(L, step))
                        if h == 0:
                            nc.vector.tensor_scalar(dst, TH[:, s, 0:w], IW[:, t, h:h + 1], 0.0, ALU.mult, ALU.add).then_inc(used.sem, note(used, step))
                        else:
                            dve.wait_ge(used.sem, used.at(L, ("I", t, h - 1)))
                            nc.vector.scalar_tensor_tensor(out=dst, in0=TH[:, s, 0:w], scalar=IW[:, t, h:h + 1], in1=dst,
                                                           op0=ALU.mult, op1=ALU.add).then_inc(used.sem, note(used, step))
                        if h == IH - 1:
                            dve.wait_ge(used.sem, used.at(L, step))
                            chain(nc.vector.tensor_tensor(dst[:, t * P:w], dst[:, t * P:w], mask(P), ALU.add))
                    elif kind in ("top", "take"):
                        _, t, r = step
                        dst = SC[:, SC_W[t]:SC_W[t] + (t + 1) * P]
                        if kind == "take":
                            dve.wait_ge(topped.sem, topped.at(L, ("top", t, r)))
                            ins = nc.vector.match_replace(dst, TOP[:], dst, TAKEN)
                        else:
                            if r > 0:
                                dve.wait_ge(topped.sem, topped.at(L, ("take", t, r - 1)))
                            elif t > 1:
                                dve.wait_ge(topped.sem, topped.at(L, ("take", t - 1, ROUNDS - 1)))
                            ins = nc.vector.max(TOP[:], dst)
                        ins.then_inc(topped.sem, note(topped, step))
                    elif kind == "KB":
                        dve.wait_ge(topped.sem, topped.at(L, ("take", NT - 1, ROUNDS - 1)))
                        chain(nc.vector.tensor_scalar(SC[:], SC[:], TAKEN / 2, MASKED, ALU.is_gt, ALU.mult))
                    elif kind == "S":
                        _, b, u = step
                        t, j, w = score_unit(b, u)
                        dve.wait_ge(s_done.sem, s_done.at(L, step))
                        if b == "A" and t > 0:
                            bias = SC[:, SC_W[t]:SC_W[t] + w]
                        elif b == "E":
                            bias = CN[:, C_MASK:C_MASK + w]
                        else:
                            bias = mask(w)
                        nc.vector.tensor_tensor_reduce(probs(b, u)[:, 0:w], S[:, 0:w], bias, -SCALE[b], -TAKEN, ALU.add, ALU.min,
                                                       NMX[:, u % 4:u % 4 + 1]).then_inc(masked.sem, note(masked, (b, u)))
                    elif kind == "V":
                        _, b, u = step
                        t, j, w = unit(b, u)
                        z = VZ[:, vz(b), t, BW:2 * BW]
                        if b != "C" and j == NH - 1:
                            dve.wait_ge(used.sem, used.at(L, (b + "1" if b != "E" else b, t)))
                            dve.wait_ge(v_done.sem, v_done.at(L, (b, u)))
                            settle()
                            chain(nc.vector.reciprocal(RI[:, 0:4], RS[:, t % 2, 0:4]))
                            chain(nc.vector.tensor_tensor(DS[:, 0:BW].rearrange("p (h c) -> p h c", h=NH),
                                                          O[:, 0:BW].rearrange("p (h c) -> p h c", h=NH),
                                                          RI[:, 0:4].unsqueeze(2).to_broadcast([P, NH, HD]), ALU.mult))
                            nc.vector.scalar_tensor_tensor(out=z, in0=DS[:, 0:BW], scalar=0.5, in1=z, op0=ALU.mult,
                                                           op1=ALU.mult).then_inc(final.sem, note(final, (b, t)))
                        if b == "C" and j == NH - 1:
                            dve.wait_ge(v_done.sem, v_done.at(L, (b, u)))
                            settle()
                            first_sums = RS[:, t % 2, :].rearrange("p (h c) -> p h c", c=2)[:, :, 0]
                            chain(nc.vector.reciprocal(RI[:, 0:4], first_sums))
                            nc.vector.tensor_tensor(DF[:].rearrange("p (h c) -> p h c", h=NH),
                                                    O[:, 0:BW].rearrange("p (h c) -> p h c", h=NH),
                                                    RI[:, 0:4].unsqueeze(2).to_broadcast([P, NH, HD]), ALU.mult).then_inc(summed.sem, note(summed, ("C", t)))
                            dve.wait_ge(summed.sem, summed.at(L, ("C", t)))
                            go(nc.vector.tensor_tensor(DS[:, 0:BW], DF[:], DF[:], ALU.mult))
                            chain(nc.vector.tensor_tensor(z, z, DF[:], ALU.mult))
                            z4 = z.rearrange("p (h c) -> p h c", h=NH)
                            nc.vector.tensor_tensor(z4, z4, DN.unsqueeze(1).to_broadcast([P, NH, HD]),
                                                    ALU.mult).then_inc(gated.sem, note(gated, ("Cz", t)))
                            nc.vector.tensor_reduce(CS[:, 0, t, :], DS[:, 0:BW].rearrange("p (h c) -> p h c", h=NH), AX.X,
                                                    ALU.add).then_inc(summed.sem, note(summed, ("Cn", t)))
                    elif kind == "lam":
                        dve.wait_ge(prm_copied.sem, prm_copied.at(L, ("prm",)))
                        dl = PRM[:, QL + KVL + HD:].rearrange("p (a b d) -> p a b d", a=2, b=2)
                        chain(nc.vector.tensor_tensor(DS[:, 0:2 * ID].rearrange("p (a d) -> p a d", a=2),
                                                      dl[:, :, 0, :], dl[:, :, 1, :], ALU.mult))
                        nc.vector.tensor_reduce(LAM[:, 0:2], DS[:, 0:2 * ID].rearrange("p (a d) -> p a d", a=2), AX.X,
                                                ALU.add).then_inc(summed.sem, note(summed, ("lam",)))
                        dve.wait_ge(rooted.sem, rooted.at(L, ("lam",)))
                        chain(nc.vector.tensor_tensor(LAM[:, 5:6], LAM[:, 3:4], LAM[:, 2:3], ALU.subtract))
                        chain(nc.vector.tensor_tensor(LAM[:, 4:5], LAM[:, 5:6], CN[:, C_LAM + L:C_LAM + L + 1], ALU.add))
                        chain(nc.vector.tensor_scalar(DN, DN,
                                                      CN[:, C_LAM + DEPTH + L:C_LAM + DEPTH + L + 1], None, ALU.mult))
                    elif kind == "W":
                        i = step[1]
                        t, j, w = unit("C", i)
                        first, second = (probs("C", 2 * i + m)[:, 0:w] for m in range(2))
                        rs = [RS[:, t % 2, 2 * j + m:2 * j + m + 1] for m in range(2)]
                        f = [CF[:, 2 * (i % 2) + m:2 * (i % 2) + m + 1] for m in range(2)]
                        dve.wait_ge(exped.sem, exped.at(L, ("C", 2 * i + 1)))
                        chain(nc.vector.reciprocal(f[0], rs[1]))
                        chain(nc.vector.scalar_tensor_tensor(out=f[1], in0=f[0], scalar=rs[0], in1=LAM[:, 4:5],
                                                             op0=ALU.mult, op1=ALU.mult))
                        nc.vector.scalar_tensor_tensor(out=first, in0=second, scalar=f[1], in1=first, op0=ALU.mult,
                                                       op1=ALU.add).then_inc(joined.sem, note(joined, step))
                    elif kind == "R":
                        dve.wait_ge(rooted.sem, rooted.at(L, ("D0",)))
                        nc.vector.reciprocal(MS[:, :, 2:4], MS[:, :, 2:4]).then_inc(inverted.sem, note(inverted, ("D0",)))
                        dve.wait_ge(rooted.sem, rooted.at(L, ("C",)))
                        nc.vector.reciprocal(CS[:, 1], CS[:, 1]).then_inc(inverted.sem, note(inverted, ("C",)))
                    elif kind == "F":
                        t = step[1]
                        z = VZ[:, 0, t, BW:2 * BW].rearrange("p (h c) -> p h c", h=NH)
                        dve.wait_ge(inverted.sem, inverted.at(L, ("C",)))
                        dve.wait_ge(gated.sem, gated.at(L, ("Cz", t)))
                        nc.vector.tensor_tensor(z, z, CS[:, 1, t, :].unsqueeze(2).to_broadcast([P, NH, HD]),
                                                ALU.mult).then_inc(final.sem, note(final, ("C", t)))
                    elif kind == "grp":
                        _, c, kh, t, part = step
                        if kh == 0 or part == 0:
                            continue
                        if c in ("A0", "B0"):
                            dve.wait_ge(copied.sem, copied.at(L, (c, t)))
                            rotate(ST[:, t, :].rearrange("p (h c) -> p h c", h=8), 8, 8, t, R64, (c, t))
                        elif c == "C0":
                            dve.wait_ge(copied.sem, copied.at(L, (c, t)))
                            rotate(ST[:, t, :].rearrange("p (h c) -> p h c", h=16), 16, 4, t, R32, (c, t))
                        elif c == "IX":
                            dve.wait_ge(copied.sem, copied.at(L, (c, t)))
                            rotate(ST[:, t, 0:288].rearrange("p (h c) -> p h c", h=9), 9, 4, t, R32, None)
                            x9 = ST[:, t, 0:(IH + 1) * ID].rearrange("p (h c) -> p h c", h=IH + 1)
                            stage = IX_STAGE[:, t]
                            st_r = stage.bitcast(F32R)
                            go(nc.vector.tensor_copy(st_r[:, 0:IH, 0:2, :], x9[:, 0:IH, :].unsqueeze(2).to_broadcast([P, IH, 2, ID])))
                            chain(nc.vector.tensor_copy(st_r[:, IH, 0:3:2, :], x9[:, IH:IH + 1, :].to_broadcast([P, 2, ID])))
                            go(nc.vector.tensor_tensor(st_r[:, 0:IH, 2, :], x9[:, 0:IH, :], stage[:, 0:IH, 0, :], ALU.subtract))
                            nc.vector.tensor_tensor(st_r[:, IH, 1, :], x9[:, IH, :], stage[:, IH, 0, :],
                                                    ALU.subtract).then_inc(roped.sem, note(roped, (c, t)))
                        elif c in ("E", "A1", "B1", "C1", "D1"):
                            s = th_n[0] % 2
                            th_n[0] += 1
                            z0 = 0 if c == "D1" else BW
                            dve.wait_ge(act_out.sem, act_out.at(L, (c, t)))
                            if c != "D1":
                                dve.wait_ge(copied.sem, copied.at(L, (c, t)))
                            nc.vector.scalar_tensor_tensor(out=VZ[:, vz(c[0]), t, BW:2 * BW], in0=TH[:, s, 0:BW], scalar=1.0,
                                                           in1=G[t][:, z0:z0 + BW], op0=ALU.add,
                                                           op1=ALU.mult).then_inc(used.sem, note(used, (c, t)))
                        elif c[0] == "g":
                            s = th_n[0] % 2
                            th_n[0] += 1
                            cc = int(c[2])
                            m = M[:, t, cc * 512:(cc + 1) * 512]
                            dve.wait_ge(act_out.sem, act_out.at(L, (c, t)))
                            dve.wait_ge(u_done.sem, u_done.at(L, (c, t)))
                            if c[1] == "E":
                                nc.vector.scalar_tensor_tensor(out=m, in0=TH[:, s, :], scalar=1.0, in1=U[:], op0=ALU.add,
                                                               op1=ALU.mult).then_inc(used.sem, note(used, (c, t)))
                            else:
                                chain(nc.vector.scalar_tensor_tensor(out=TH[:, s, :], in0=TH[:, s, :], scalar=1.0, in1=U[:],
                                                                     op0=ALU.add, op1=ALU.mult))
                                nc.vector.tensor_tensor(m, m, TH[:, s, :], ALU.add).then_inc(used.sem, note(used, (c, t)))
                        elif c[0] == "O":
                            cc = int(c[1])
                            xc = X[:, t, cc * 512:(cc + 1) * 512]
                            dve.wait_ge(gemm.sem, gemm.at(L, (c, 1, t)))
                            nc.vector.scalar_tensor_tensor(out=xc, in0=G[t][:], scalar=0.5 / ALPHA, in1=xc, op0=ALU.mult,
                                                           op1=ALU.add).then_inc(residual.sem, note(residual, (c, t)))
                            dve.wait_ge(residual.sem, residual.at(L, (c, t)))
                            if cc == 0:
                                go(half_stats(t, 0))
                            else:
                                if t == 0:
                                    dve.wait_ge(ln_in.sem, ln_in.at(L, ("ln",)))
                                stats(t, ("ln", t))


_INS = ["x", "mem", "ln0_g", "ln0_b", "w_in", "mla_q_norm", "w_uq", "mla_kv_norm", "w_ukv", "diff_lam",
        "diff_norm", "w_mem_kv", "w_branch", "w_out", "ln_g", "ln_b"]


def kernel(**inputs):
    import numpy as _np
    import concourse.bacc as _bacc
    from concourse import mybir as _mybir
    from concourse.bass_utils import run_bass_kernel_spmd as _run

    arrays = {f"in_{name}_dram": _np.ascontiguousarray(inputs[name]) for name in _INS}
    arrays["shape_constants_dram"] = constants()
    known = {}
    for _ in range(2):
        nc = _bacc.Bacc("TRN2", target_bir_lowering=False, num_devices=1)
        args = [nc.dram_tensor(name, a.shape, _mybir.dt.from_np(a.dtype), kind="ExternalInput").ap()
                for name, a in arrays.items()]
        args.append(nc.dram_tensor("out_0_dram", (1, T, D), _mybir.dt.float32, kind="ExternalOutput").ap())
        build(nc, known, *args)
    r = _run(nc, [arrays], core_ids=[0])
    return r.results[0]["out_0_dram"]
```
